# Optimizing a Trainium2 kernel written in Bass

```python
import jax, jax.numpy as jnp
from jax import lax
import numpy as np

D_MODEL = 1024
BATCH = 1
SEQ = 2048
DEPTH = 1

CHUNK = 64
HEAD_DIM = 64
ROPE_THETA = 10000.0
NORM_EPS = 1e-6
NEG_INF = -1e30
A_Q_HEADS = 8
A_KV_HEADS = 2
A_GROUP = A_Q_HEADS // A_KV_HEADS
A_WINDOW = 128
A_BAND_CHUNKS = A_WINDOW // CHUNK
B_HEADS = 8
B_LEFT_CHUNKS = 8
B_BAND_CHUNKS = B_LEFT_CHUNKS + 1
B_MAX_REL = 256
N_BRANCHES = 2
A_Q_W = A_Q_HEADS * HEAD_DIM
A_KV_W = A_KV_HEADS * HEAD_DIM
B_W = B_HEADS * HEAD_DIM
IN_W = A_Q_W + 2 * A_KV_W + 3 * B_W
N_GROUPS = 4
EXPERTS_PER_GROUP = 8
N_EXPERTS = N_GROUPS * EXPERTS_PER_GROUP
TOP_K_IN_GROUP = 2
D_EXPERT = 512
MOE_BLOCK = 256

kernel_name = "hybrid_chunk_causal_swa_relbias_hmoe"

def rmsnorm(x, g):
    x32 = x.astype(jnp.float32)
    y = x32 * lax.rsqrt(jnp.mean(x32 * x32, axis=-1, keepdims=True) + NORM_EPS)
    return (y * g.astype(jnp.float32)).astype(x.dtype)

def rope(t, pos):
    half = t.shape[-1] // 2
    inv = ROPE_THETA ** (-jnp.arange(half, dtype=jnp.float32) / half)
    ang = pos.astype(jnp.float32)[:, None] * inv[None, :]
    cos = jnp.cos(ang)[None, :, None, :]
    sin = jnp.sin(ang)[None, :, None, :]
    t1 = t[..., :half].astype(jnp.float32)
    t2 = t[..., half:].astype(jnp.float32)
    return jnp.concatenate([t1 * cos - t2 * sin, t2 * cos + t1 * sin], axis=-1).astype(t.dtype)

def chunk_band(t, n_band):
    b, nc = t.shape[:2]
    pad = jnp.zeros((b, n_band - 1) + t.shape[2:], t.dtype)
    tp = jnp.concatenate([pad, t], axis=1)
    idx = jnp.arange(nc)[:, None] + jnp.arange(n_band)[None, :]
    band = tp[:, idx]
    return band.reshape((b, nc, n_band * t.shape[2]) + t.shape[3:])

def band_valid(nc, n_band):
    chunk_ids = jnp.arange(nc)[:, None] + jnp.arange(n_band)[None, :] - (n_band - 1)
    return jnp.repeat(chunk_ids >= 0, CHUNK, axis=1)

def swa_gqa_sinks(q, k, v, sinks):
    b, s = q.shape[:2]
    nc = s // CHUNK
    qc = q.reshape(b, nc, CHUNK, A_KV_HEADS, A_GROUP, HEAD_DIM)
    kb = chunk_band(k.reshape(b, nc, CHUNK, A_KV_HEADS, HEAD_DIM), A_BAND_CHUNKS)
    vb = chunk_band(v.reshape(b, nc, CHUNK, A_KV_HEADS, HEAD_DIM), A_BAND_CHUNKS)
    scores = jnp.einsum('bnqkgd,bnskd->bnkgqs', qc, kb,
                        preferred_element_type=jnp.float32) * (HEAD_DIM ** -0.5)
    valid = band_valid(nc, A_BAND_CHUNKS)
    scores = jnp.where(valid[None, :, None, None, None, :], scores, NEG_INF)
    sink = sinks.astype(jnp.float32).reshape(1, 1, A_KV_HEADS, A_GROUP, 1, 1)
    m = jnp.maximum(jnp.max(scores, axis=-1, keepdims=True), sink)
    p = jnp.exp(scores - m)
    probs = (p / (jnp.sum(p, axis=-1, keepdims=True) + jnp.exp(sink - m))).astype(v.dtype)
    out = jnp.einsum('bnkgqs,bnskd->bnqkgd', probs, vb)
    return out.reshape(b, s, A_Q_W)

def chunk_relbias_attention(q, k, v, rel_bias):
    b, s = q.shape[:2]
    nc = s // CHUNK
    qc = q.reshape(b, nc, CHUNK, B_HEADS, HEAD_DIM)
    kb = chunk_band(k.reshape(b, nc, CHUNK, B_HEADS, HEAD_DIM), B_BAND_CHUNKS)
    vb = chunk_band(v.reshape(b, nc, CHUNK, B_HEADS, HEAD_DIM), B_BAND_CHUNKS)
    scores = jnp.einsum('bnqhd,bnshd->bnhqs', qc, kb,
                        preferred_element_type=jnp.float32) * (HEAD_DIM ** -0.5)
    dist = jnp.arange(CHUNK)[:, None] - (jnp.arange(B_BAND_CHUNKS * CHUNK)[None, :] - B_LEFT_CHUNKS * CHUNK)
    idx = jnp.clip(dist, -B_MAX_REL, B_MAX_REL) + B_MAX_REL
    bias = rel_bias[:, idx].astype(jnp.float32)
    scores = scores + bias[None, None]
    valid = band_valid(nc, B_BAND_CHUNKS)
    scores = jnp.where(valid[None, :, None, None, :], scores, NEG_INF)
    probs = jax.nn.softmax(scores, axis=-1).astype(v.dtype)
    out = jnp.einsum('bnhqs,bnshd->bnqhd', probs, vb)
    return out.reshape(b, s, B_W)

def hierarchical_moe(h, w_rg, b_rg, w_re, b_re, w_eg, w_eu, w_ed):
    b, s, d = h.shape
    n = b * s
    hf = h.reshape(n, d)
    g_logits = jnp.dot(hf, w_rg, preferred_element_type=jnp.float32) + b_rg.astype(jnp.float32)
    e_logits = jnp.dot(hf, w_re, preferred_element_type=jnp.float32) + b_re.astype(jnp.float32)
    g_prob = jax.nn.softmax(g_logits, axis=-1)
    g_sel = jnp.argmax(g_logits, axis=-1)
    p_group = jnp.take_along_axis(g_prob, g_sel[:, None], axis=-1)
    in_logits = jnp.take_along_axis(e_logits.reshape(n, N_GROUPS, EXPERTS_PER_GROUP),
                                    g_sel[:, None, None], axis=1)[:, 0]
    top_v, top_i = lax.top_k(in_logits, TOP_K_IN_GROUP)
    gate_w = p_group * jax.nn.softmax(top_v, axis=-1)
    expert_id = g_sel[:, None] * EXPERTS_PER_GROUP + top_i

    nk = n * TOP_K_IN_GROUP
    cap = nk + N_EXPERTS * MOE_BLOCK
    n_blocks = cap // MOE_BLOCK
    flat_e = expert_id.reshape(nk).astype(jnp.int32)
    flat_tok = jnp.repeat(jnp.arange(n, dtype=jnp.int32), TOP_K_IN_GROUP)
    flat_w = gate_w.reshape(nk)
    order = jnp.argsort(flat_e, stable=True)
    sorted_e = flat_e[order]
    counts = jnp.bincount(flat_e, length=N_EXPERTS)
    starts = jnp.cumsum(counts) - counts
    pcounts = ((counts + MOE_BLOCK - 1) // MOE_BLOCK) * MOE_BLOCK
    pends = jnp.cumsum(pcounts)
    pstarts = pends - pcounts
    dest = pstarts[sorted_e] + (jnp.arange(nk, dtype=jnp.int32) - starts[sorted_e])
    row_tok = jnp.zeros((cap,), jnp.int32).at[dest].set(flat_tok[order])
    row_w = jnp.zeros((cap,), jnp.float32).at[dest].set(flat_w[order])
    block_e = jnp.clip(jnp.searchsorted(pends, jnp.arange(n_blocks) * MOE_BLOCK, side='right'),
                       0, N_EXPERTS - 1)
    xs = hf[row_tok].reshape(n_blocks, MOE_BLOCK, d)

    def expert_block(args):
        xb, e = args
        a = jax.nn.silu(xb @ w_eg[e]) * (xb @ w_eu[e])
        return a @ w_ed[e]

    ys = lax.map(expert_block, (xs, block_e)).reshape(cap, d)
    ys = ys * row_w[:, None].astype(ys.dtype)
    out = jnp.zeros((n, d), h.dtype).at[row_tok].add(ys.astype(h.dtype))
    return out.reshape(b, s, d)

def setup_inputs(seed: int = 0) -> dict:
    key = jax.random.key(seed)
    ks = jax.random.split(key, 20)
    f32 = jnp.float32
    nrm = lambda k, shape, scale: (jax.random.normal(k, shape, f32) * scale).astype(f32)
    return {
        "x": nrm(ks[0], (BATCH, SEQ, D_MODEL), 1.0),
        "norm_mix": 1.0 + nrm(ks[1], (DEPTH, D_MODEL), 0.02),
        "w_in": nrm(ks[2], (DEPTH, D_MODEL, IN_W), D_MODEL ** -0.5),
        "attn_sinks": nrm(ks[3], (DEPTH, A_Q_HEADS), 0.5),
        "rel_bias": nrm(ks[4], (DEPTH, B_HEADS, 2 * B_MAX_REL + 1), 0.1),
        "w_o_a": nrm(ks[5], (DEPTH, A_Q_W, D_MODEL), A_Q_W ** -0.5),
        "w_o_b": nrm(ks[6], (DEPTH, B_W, D_MODEL), B_W ** -0.5),
        "w_branch_gate": nrm(ks[7], (DEPTH, D_MODEL, N_BRANCHES * D_MODEL), D_MODEL ** -0.5),
        "b_branch_gate": nrm(ks[8], (DEPTH, N_BRANCHES * D_MODEL), 0.1),
        "w_out": nrm(ks[9], (DEPTH, D_MODEL, D_MODEL), D_MODEL ** -0.5),
        "norm_ffn": 1.0 + nrm(ks[10], (DEPTH, D_MODEL), 0.02),
        "w_router_group": nrm(ks[11], (DEPTH, D_MODEL, N_GROUPS), D_MODEL ** -0.5),
        "b_router_group": nrm(ks[12], (DEPTH, N_GROUPS), 0.01),
        "w_router_expert": nrm(ks[13], (DEPTH, D_MODEL, N_EXPERTS), D_MODEL ** -0.5),
        "b_router_expert": nrm(ks[14], (DEPTH, N_EXPERTS), 0.01),
        "w_exp_gate": nrm(ks[15], (DEPTH, N_EXPERTS, D_MODEL, D_EXPERT), D_MODEL ** -0.5),
        "w_exp_up": nrm(ks[16], (DEPTH, N_EXPERTS, D_MODEL, D_EXPERT), D_MODEL ** -0.5),
        "w_exp_down": nrm(ks[17], (DEPTH, N_EXPERTS, D_EXPERT, D_MODEL), D_EXPERT ** -0.5),
        "norm_final": 1.0 + nrm(ks[18], (D_MODEL,), 0.02),
    }

def reference(x, norm_mix, w_in, attn_sinks, rel_bias, w_o_a, w_o_b, w_branch_gate,
              b_branch_gate, w_out, norm_ffn, w_router_group, b_router_group,
              w_router_expert, b_router_expert, w_exp_gate, w_exp_up, w_exp_down, norm_final):
    b, s, d = x.shape
    pos = jnp.arange(s, dtype=jnp.int32)
    splits = np.cumsum([A_Q_W, A_KV_W, A_KV_W, B_W, B_W])
    for l in range(DEPTH):
        h = rmsnorm(x, norm_mix[l])
        proj = h @ w_in[l]
        qa, ka, va, qb, kb, vb = jnp.split(proj, splits, axis=-1)
        qa = rope(qa.reshape(b, s, A_Q_HEADS, HEAD_DIM), pos)
        ka = rope(ka.reshape(b, s, A_KV_HEADS, HEAD_DIM), pos)
        va = va.reshape(b, s, A_KV_HEADS, HEAD_DIM)
        ya = swa_gqa_sinks(qa, ka, va, attn_sinks[l]) @ w_o_a[l]
        yb = chunk_relbias_attention(qb.reshape(b, s, B_HEADS, HEAD_DIM),
                                     kb.reshape(b, s, B_HEADS, HEAD_DIM),
                                     vb.reshape(b, s, B_HEADS, HEAD_DIM),
                                     rel_bias[l]) @ w_o_b[l]
        gates = jax.nn.sigmoid(h @ w_branch_gate[l] + b_branch_gate[l]).reshape(b, s, N_BRANCHES, d)
        mixed = gates[:, :, 0] * ya + gates[:, :, 1] * yb
        x = x + mixed @ w_out[l]
        h2 = rmsnorm(x, norm_ffn[l])
        x = x + hierarchical_moe(h2, w_router_group[l], b_router_group[l],
                                 w_router_expert[l], b_router_expert[l],
                                 w_exp_gate[l], w_exp_up[l], w_exp_down[l])
    return rmsnorm(x, norm_final)


_drawn_inputs = setup_inputs


def setup_inputs(seed=0):
    import zlib

    import numpy as np

    out = dict(_drawn_inputs(seed))
    spreads = {}
    factors = {'norm_mix': 3.751,
     'attn_sinks': 64.0,
     'rel_bias': 4.447,
     'b_branch_gate': 4.227,
     'b_router_group': 19.355,
     'b_router_expert': 24.771,
     'norm_final': 8.441,
     'norm_ffn': 6.439}
    for name, (base, spread) in spreads.items():
        noise = np.random.default_rng([zlib.crc32(name.encode()), seed]).standard_normal(out[name].shape)
        drawn = base * np.exp(spread * noise) if base else spread * noise
        out[name] = __import__('jax').numpy.asarray(drawn.astype(out[name].dtype))
    for name, factor in factors.items():
        out[name] = (out[name] * factor).astype(out[name].dtype)
    return out
```

```python
from contextlib import ExitStack

import numpy as np

import concourse.bass as bass
from concourse import mybir

ALU = mybir.AluOpType
ACT = mybir.ActivationFunctionType
AX_X = mybir.AxisListType.X
F32 = mybir.dt.float32
F32R = mybir.dt.float32r
BF16 = mybir.dt.bfloat16
I32 = mybir.dt.int32
U32 = mybir.dt.uint32
ds = bass.ds

P = 128
SEQ = 2048
D = 1024
KD = D // P
NT = SEQ // P
EPS = 1e-6
NEG = -1e30
NB = 512
COPY_TILES = 18
GATE_TILES = 16
ROPE_FIRST = 12
ROPE_TILES = 5
HALF = SEQ // 2
A_COLS = 512
CHUNK = 64
MAX_REL = 256


class Stage:

    def __init__(self, nc, tag):
        self.nc, self.tag, self.ctx, self.sems = nc, tag, ExitStack(), []

    def __enter__(self):
        return self

    def __exit__(self, *exc):
        self.ctx.close()
        if self.sems:
            self.nc.clear_and_free_semaphores(self.sems)
            self.nc.all_engine_barrier()

    def sb(self, name, shape, dt=F32):
        return self.ctx.enter_context(self.nc.sbuf_tensor(f"{self.tag}_{name}", shape, dt))

    def ps(self, name, shape, dt=F32):
        return self.ctx.enter_context(self.nc.psum_tensor(f"{self.tag}_{name}", shape, dt))

    def sem(self, name):
        self.sems.append(self.nc.alloc_semaphore(f"{self.tag}_{name}"))
        return self.sems[-1]

    def block(self):
        return self.ctx.enter_context(self.nc.Block())


def hold(eng, spare):
    eng.sem_inc(spare, 1)


def rms_tail(dve, stat, t, ssq_done, mean_done, root_done, rstd_done):
    dve.wait_ge(ssq_done, t + 1)
    dve.tensor_scalar(stat[:, 1:2], stat[:, 0:1], 1.0 / D, EPS, ALU.mult, ALU.add).then_inc(mean_done, 1)
    dve.wait_ge(root_done, t + 1)
    newton(dve, stat, t, rstd_done)


def newton(dve, stat, t, rstd_done):
    dve.reciprocal(stat[:, 3:4], stat[:, 2:3]).then_inc(rstd_done, 1)
    dve.wait_ge(rstd_done, t * 4 + 1)
    dve.scalar_tensor_tensor(stat[:, 4:5], stat[:, 3:4], stat[:, 3:4], stat[:, 1:2],
                             ALU.mult, ALU.mult).then_inc(rstd_done, 1)
    dve.wait_ge(rstd_done, t * 4 + 2)
    dve.tensor_scalar(stat[:, 5:6], stat[:, 4:5], -0.5, 1.5, ALU.mult, ALU.add).then_inc(rstd_done, 1)
    dve.wait_ge(rstd_done, t * 4 + 3)
    dve.tensor_tensor(stat[:, 6:7], stat[:, 3:4], stat[:, 5:6], ALU.mult).then_inc(rstd_done, 1)
    dve.wait_ge(rstd_done, t * 4 + 4)


def project(nc, x, norm_mix, w_feat, gate_bias, rope_cos, rope_sin, ident, feat, rotated, gates):
    with Stage(nc, "pj") as st:
        hT_hi = st.sb("hT_hi", [P, KD, SEQ], F32R)
        hT_lo = st.sb("hT_lo", [P, KD, SEQ], F32R)
        x_in = [st.sb(f"x_in{p}", [P, D]) for p in range(2)]
        h_tok = x_in
        w_raw = [st.sb(f"w_raw{p}", [P, D]) for p in range(2)]
        w_hi = [st.sb(f"w_hi{p}", [P, D], F32R) for p in range(2)]
        w_lo = [st.sb(f"w_lo{p}", [P, D], F32R) for p in range(2)]
        f_out = [st.sb(f"f_out{p}", [P, HALF]) for p in range(2)]
        g_row = st.sb("g_row", [P, D])
        idt = st.sb("idt", [P, P])
        ro_raw, ro_swap, ro_cos, ro_sin, ro_out = (
            st.sb(n, [P, NB]) for n in ("ro_raw", "ro_swap", "ro_cos", "ro_sin", "ro_out"))
        gbias = st.sb("gbias", [P, GATE_TILES])
        stat = [st.sb(f"stat{p}", [P, 8]) for p in range(2)]
        eight = [st.ps(f"bank{b}", [P, NB]) for b in range(8)]

        junk = [st.sb(f"junk{p}", [P, D], BF16) for p in range(2)]
        held = st.sem("held")
        const_in = st.sem("const_in")
        x_ready = [st.sem(f"x_ready{p}") for p in range(2)]
        ssq_done = st.sem("ssq_done")
        mean_done = st.sem("mean_done")
        root_done = st.sem("root_done")
        rstd_done = st.sem("rstd_done")
        h_done = st.sem("h_done")
        tr_done = st.sem("tr_done")
        hi_done = st.sem("hi_done")
        tr_read = st.sem("tr_read")
        w_ready = [st.sem(f"w_ready{p}") for p in range(2)]
        whi_done = st.sem("whi_done")
        wlo_done = st.sem("wlo_done")
        mm_done = st.sem("mm_done")
        evacuated = st.sem("evacuated")
        stored = [st.sem(f"stored{p}") for p in range(2)]
        ro_in, ro_done, ro_stored = st.sem("ro_in"), st.sem("ro_done"), st.sem("ro_stored")
        block = st.block()
        TILES = COPY_TILES + GATE_TILES

        @block.sync
        def _(sp):
            sp.dma_start(g_row[:], norm_mix.partition_broadcast(P)).then_inc(const_in, 16)
            sp.dma_start(idt[:], ident).then_inc(const_in, 16)
            sp.dma_start(gbias[:], gate_bias).then_inc(const_in, 16)
            for p in range(2):
                sp.dma_start(x_in[p][:], x[p * P:(p + 1) * P, :]).then_inc(x_ready[p], 16)
            for p in range(2):
                sp.dma_start(w_raw[p][:], w_feat[p]).then_inc(w_ready[p], 16)
            with sp.Fori(1, NT // 2) as i:
                for p in range(2):
                    sp.wait_ge(tr_done, i * 2 + p - 1)
                    sp.dma_start(x_in[p][:], x[ds((i * 2 + p) * P, P), :]).then_inc(x_ready[p], 16)

            def store(dst, i, first, more=True):
                for p in range(2):
                    if more:
                        sp.wait_ge(wlo_done, i * 2 + p + first + 1)
                        sp.dma_start(w_raw[p][:], w_feat[ds(i * 2 + p + first + 2, 1), :, :].rearrange(
                            "a p n -> (a p) n")).then_inc(w_ready[p], 16)
                    for half in range(2):
                        sp.wait_ge(evacuated, (i * 2 + p + first) * 4 + 8 + 2 * half + 2)
                        sp.dma_start(dst[ds(i * 2 + p, 1), :, half * HALF:(half + 1) * HALF]
                                     .rearrange("a p n -> (a p) n"), f_out[half][:]).then_inc(stored[half], 16)

            with sp.Fori(0, COPY_TILES // 2) as i:
                store(feat, i, 0)
            with sp.Fori(0, GATE_TILES // 2 - 1) as i:
                store(gates, i, COPY_TILES)
            with sp.Fori(GATE_TILES // 2 - 1, GATE_TILES // 2) as i:
                store(gates, i, COPY_TILES, more=False)
            for half in range(2):
                sp.wait_ge(stored[half], 16 * TILES)

        @block.gpsimd
        def _(pool):
            for r in range(ROPE_TILES):
                for half in range(2):
                    pool.wait_ge(stored[half], 16 * (ROPE_FIRST + r + 1))
                with pool.Fori(0, SEQ // NB) as c:
                    cols = ds(c * NB, NB)
                    pool.wait_ge(ro_stored, (c + r * (SEQ // NB)) * 16)
                    pool.dma_start(ro_raw[:], feat[ROPE_FIRST + r, :, cols]).then_inc(ro_in, 16)
                    for q in range(4):
                        src = (q ^ 1) * 32
                        pool.dma_start(ro_swap[q * 32:q * 32 + 32, :],
                                       feat[ROPE_FIRST + r, src:src + 32, cols]).then_inc(ro_in, 16)
                    pool.dma_start(ro_cos[:], rope_cos[:, cols]).then_inc(ro_in, 16)
                    pool.dma_start(ro_sin[:], rope_sin[:, cols]).then_inc(ro_in, 16)
                    pool.wait_ge(ro_in, (c + r * (SEQ // NB)) * 112 + 112)
                    pool.tensor_tensor(ro_out[:], ro_raw[:], ro_cos[:], ALU.mult).then_inc(ro_done, 1)
                    pool.tensor_tensor(ro_swap[:], ro_swap[:], ro_sin[:], ALU.mult).then_inc(ro_done, 1)
                    pool.wait_ge(ro_done, (c + r * (SEQ // NB)) * 3 + 2)
                    pool.tensor_tensor(ro_out[:], ro_out[:], ro_swap[:], ALU.add).then_inc(ro_done, 1)
                    pool.wait_ge(ro_done, (c + r * (SEQ // NB)) * 3 + 3)
                    hold(pool, held)
                    pool.dma_start(rotated[r * P:(r + 1) * P, cols], ro_out[:]).then_inc(ro_stored, 16)
            pool.wait_ge(ro_stored, ROPE_TILES * (SEQ // NB) * 16)

        @block.scalar
        def _(act):
            with act.Fori(0, NT // 2) as i:
                for p in range(2):
                    act.wait_ge(x_ready[p], i * 16 + 16)
                    act.activation(junk[p][:], x_in[p][:], ACT.Square, accum_out=stat[p][:, 0:1]).then_inc(ssq_done, 1)
                for p in range(2):
                    act.wait_ge(mean_done, i * 2 + p + 1)
                    act.activation(stat[p][:, 2:3], stat[p][:, 1:2], ACT.Sqrt).then_inc(root_done, 1)
                for p in range(2):
                    act.wait_ge(tr_done, i * 2 + p + 1)
                    hold(act, held)
                    for b in range(2):
                        act.activation(hT_hi[:, 4 * b:4 * b + 4, ds((i * 2 + p) * P, P)],
                                       eight[2 * p + b][:].rearrange("p (k t) -> p k t", k=4),
                                       ACT.Copy).then_inc(hi_done, 1)

            def split_weights(i, p):
                act.wait_ge(w_ready[p], i * 16 + 16)
                act.wait_ge(mm_done, i * 2 + p + 1)
                act.activation(w_hi[p][:], w_raw[p][:], ACT.Copy).then_inc(whi_done, 1)

            def evacuate(i, p, first, func):
                act.wait_ge(mm_done, i * 2 + p + first + 3)
                for half in range(2):
                    act.wait_ge(stored[half], (i * 2 + p + first) * 16)
                    if func == ACT.Sigmoid:
                        hold(act, held)
                    for b in range(2):
                        bias = gbias[:, ds(i * 2 + p, 1)] if func == ACT.Sigmoid else 0.0
                        act.activation(f_out[half][:, b * NB:(b + 1) * NB], eight[4 * p + 2 * half + b][:],
                                       func, bias=bias).then_inc(evacuated, 1)

            split_weights(0, 0)
            split_weights(0, 1)
            with act.Fori(0, COPY_TILES // 2) as i:
                for p in range(2):
                    evacuate(i, p, 0, ACT.Copy)
                    split_weights(i + 1, p)
            act.wait_ge(const_in, 48)
            with act.Fori(0, GATE_TILES // 2 - 1) as i:
                for p in range(2):
                    evacuate(i, p, COPY_TILES, ACT.Sigmoid)
                    split_weights(i + (COPY_TILES // 2 + 1), p)
            with act.Fori(GATE_TILES // 2 - 1, GATE_TILES // 2) as i:
                for p in range(2):
                    evacuate(i, p, COPY_TILES, ACT.Sigmoid)

        @block.vector
        def _(dve):
            dve.wait_ge(const_in, 48)
            with dve.Fori(0, NT // 2) as i:
                for p in range(2):
                    dve.wait_ge(ssq_done, i * 2 + p + 1)
                    dve.tensor_scalar(stat[p][:, 1:2], stat[p][:, 0:1], 1.0 / D, EPS,
                                      ALU.mult, ALU.add).then_inc(mean_done, 1)
                for p in range(2):
                    dve.wait_ge(root_done, i * 2 + p + 1)
                    newton(dve, stat[p], i * 2 + p, rstd_done)
                    dve.scalar_tensor_tensor(x_in[p][:], x_in[p][:], stat[p][:, 6:7], g_row[:],
                                             ALU.mult, ALU.mult).then_inc(h_done, 1)
                for p in range(2):
                    for b in range(2):
                        dve.wait_ge(hi_done, i * 4 + 2 * p + b + 1)
                        where = (slice(None), slice(4 * b, 4 * b + 4), ds((i * 2 + p) * P, P))
                        dve.tensor_tensor(hT_lo[where], eight[2 * p + b][:].rearrange("p (k t) -> p k t", k=4),
                                          hT_hi[where], ALU.subtract).then_inc(tr_read, 1)
            with dve.Fori(0, TILES // 2) as i:
                for p in range(2):
                    dve.wait_ge(whi_done, i * 2 + p + 1)
                    dve.tensor_tensor(w_lo[p][:], w_raw[p][:], w_hi[p][:], ALU.subtract).then_inc(wlo_done, 1)

        @block.tensor
        def _(pe):
            pe.sem_inc(tr_read, 4)
            pe.sem_inc(mm_done, 2)
            pe.sem_inc(evacuated, 8)
            pe.wait_ge(const_in, 48)
            with pe.Fori(0, NT // 2) as i:
                for p in range(2):
                    pe.wait_ge(h_done, i * 2 + p + 1)
                    pe.wait_ge(tr_read, i * 4 + 2 * p + 2)
                    for k in range(KD):
                        last = pe.transpose(eight[2 * p + k // 4][:, (k % 4) * P:(k % 4 + 1) * P],
                                            x_in[p][:, k * P:(k + 1) * P], idt[:])
                    last.then_inc(tr_done, 1)
            pe.wait_ge(tr_read, 2 * NT + 4)
            with pe.Fori(0, TILES // 2) as i:
                for p in range(2):
                    pe.wait_ge(wlo_done, i * 2 + p + 1)
                    pe.wait_ge(evacuated, (i * 2 + p) * 4 + 4)
                    for k in range(KD):
                        for n, (w, h) in enumerate(((w_hi, hT_hi), (w_hi, hT_lo), (w_lo, hT_hi))):
                            for b in range(4):
                                last = pe.matmul(eight[4 * p + b][:], w[p][:, k * P:(k + 1) * P],
                                                 h[:, k, b * NB:(b + 1) * NB],
                                                 start=(k == 0 and n == 0), stop=(k == KD - 1 and n == 2))
                    last.then_inc(mm_done, 1)


HEADS = 8
DH = 64
NPAIR = HEADS // 2
UNITS = 2 * NT


def attend(nc, tag, q_rows, k_rows, v_rows, head_of, shared_kv, key_tiles, bias, sinks, ident, att, att_col, blank=None):
    KW = key_tiles * P
    with Stage(nc, tag) as st:
        k_raw = st.sb("k_raw", [P, SEQ])
        q_raw = st.sb("q_raw", [P, SEQ])
        v_raw = st.sb("v_raw", [DH, SEQ])
        k_st = [st.sb(f"k_st{p}", [P, SEQ], F32R) for p in range(2)]
        q_hi = [st.sb(f"q_hi{p}", [P, SEQ], F32R) for p in range(2)]
        q_lo = [st.sb(f"q_lo{p}", [P, SEQ], F32R) for p in range(2)]
        v_st = [st.sb(f"v_st{p}", [P, NT, 2, DH], F32R) for p in range(2)]
        bias_sb = [st.sb(f"bias{p}", [P, KW]) for p in range(2)]
        prob = [st.sb(f"prob{p}", [P, KW]) for p in range(3)]
        pt_hi = [st.sb(f"pt_hi{p}", [P, KW], F32R) for p in range(2)]
        pt_lo = [st.sb(f"pt_lo{p}", [P, KW], F32R) for p in range(2)]
        o_head = [st.sb(f"o_head{p}", [P, NT, DH]) for p in range(2)]
        idt = st.sb("idt", [P, P])
        sink = st.sb("sink", [P, HEADS])
        top = st.sb("top", [P, UNITS])
        neg = st.sb("neg", [P, UNITS])
        total = st.sb("total", [P, UNITS])
        sink_p = st.sb("sink_p", [P, UNITS])
        full = st.sb("full", [P, UNITS])
        inv = st.sb("inv", [P, UNITS])
        s_ps = [st.ps(f"s_ps{p}", [P, 2 * NB]) for p in range(2)]
        pt_ps = st.ps("pt_ps", [P, 2 * NB])
        o_ps = [st.ps(f"o_ps{p}", [P, NB]) for p in range(2)]
        v_ps = pt_ps[:].rearrange("p (n d) -> p n d", d=DH)

        held = st.sem("held")
        const_in = st.sem("const_in")
        q_in = st.sem("q_in")
        kv_in = st.sem("kv_in")
        q_hi_done = st.sem("q_hi_done")
        q_lo_done = st.sem("q_lo_done")
        k_hi_done = st.sem("k_hi_done")
        k_lo_done = st.sem("k_lo_done")
        v_tr = st.sem("v_tr")
        v_hi_done = st.sem("v_hi_done")
        v_lo_done = st.sem("v_lo_done")
        scored = st.sem("scored")
        maxed = st.sem("maxed")
        neg_done = st.sem("neg_done")
        exped = st.sem("exped")
        sink_done = st.sem("sink_done")
        transposed = st.sem("transposed")
        pt_hi_done = st.sem("pt_hi_done")
        pt_lo_done = st.sem("pt_lo_done")
        valued = st.sem("valued")
        full_done = st.sem("full_done")
        inv_done = st.sem("inv_done")
        o_done = st.sem("o_done")
        att_out = [st.sem(f"att_out{p}") for p in range(2)]
        block = st.block()
        with_sink = sinks is not None
        kv_heads = 2 if shared_kv else HEADS
        CONSTS = 16 * (1 + with_sink + 2 * shared_kv)

        def tiles_of(n):
            m = min(n + 1, key_tiles)
            return n + 1 - m, m

        @block.sync
        def _(sp):
            def load_q(pair, hh):
                for half in range(2):
                    sp.dma_start(q_raw[half * DH:(half + 1) * DH, :], q_rows(pair, hh)).then_inc(q_in, 16)
                if not shared_kv:
                    sp.dma_start(bias_sb[hh][:], bias(pair, hh)).then_inc(q_in, 16)

            def load_kv(pair, hh):
                for half in range(2):
                    sp.dma_start(k_raw[half * DH:(half + 1) * DH, :], k_rows(pair, hh)).then_inc(kv_in, 16)
                sp.dma_start(v_raw[:], v_rows(pair, hh)).then_inc(kv_in, 16)

            sp.dma_start(idt[:], ident).then_inc(const_in, 16)
            if with_sink:
                sp.dma_start(sink[:], sinks.partition_broadcast(P)).then_inc(const_in, 16)
            if shared_kv:
                for p in range(2):
                    sp.dma_start(bias_sb[p][:], bias(0, p)).then_inc(const_in, 16)
            load_kv(0, 0)
            load_q(0, 0)
            if shared_kv:
                sp.wait_ge(k_lo_done, 1)
                sp.wait_ge(v_tr, 1)
                load_kv(0, 1)
            with sp.Fori(0, NPAIR) as j:
                for hh in range(2):
                    sp.wait_ge(q_lo_done, j * 2 + hh + 1)
                    if not shared_kv:
                        sp.wait_ge(k_lo_done, j * 2 + hh + 1)
                        sp.wait_ge(v_tr, j * 2 + hh + 1)
                        sp.wait_ge(maxed, (j * 2 + hh) * NT + 2)
                    nj, nh = (j, 1) if hh == 0 else (j + 1, 0)
                    hold(sp, held)
                    load_q(nj, nh)
                    if not shared_kv:
                        load_kv(nj, nh)
                    sp.wait_ge(o_done, (j * 2 + hh) * NT + NT + 2)
                    hold(sp, held)
                    dst = att[:SEQ, ds(head_of(j, hh) * DH + att_col, DH)].rearrange("(n p) d -> p n d", p=P)
                    sp.dma_start(dst, o_head[hh][:]).then_inc(att_out[hh], 16)
            for hh in range(2):
                sp.wait_ge(att_out[hh], 16 * NPAIR)
            sp.wait_ge(q_in, (HEADS + 1) * 16 * (2 if shared_kv else 3))
            sp.wait_ge(kv_in, (2 if shared_kv else HEADS + 1) * 48)

        if blank is not None:
            zeros = st.sb("zeros", [P, D])
            zeros_set, blanked = st.sem("zeros_set"), st.sem("blanked")

            @block.gpsimd
            def _(pool):
                pool.memset(zeros[:], 0.0).then_inc(zeros_set, 1)
                pool.wait_ge(zeros_set, 1)
                tiles = sum(rows.shape[0] for rows in blank) // P
                for rows in blank:
                    with pool.Fori(0, rows.shape[0] // P) as t:
                        pool.dma_start(rows[ds(t * P, P), :], zeros[:]).then_inc(blanked, 16)
                pool.wait_ge(blanked, tiles * 16)

        @block.scalar
        def _(act):
            def split_q(h, hh):
                act.wait_ge(q_in, (h + 1) * (32 if shared_kv else 48))
                act.activation(q_hi[hh][:], q_raw[:], ACT.Copy, scale=0.125).then_inc(q_hi_done, 1)

            def split_k(h, hh):
                act.wait_ge(kv_in, (h + 1) * 48)
                act.activation(k_st[hh][:], k_raw[:], ACT.Copy).then_inc(k_hi_done, 1)

            def split_v(h, hh):
                act.wait_ge(v_tr, h + 1)
                act.activation(v_st[hh][:, :, 0, :], v_ps, ACT.Copy).then_inc(v_hi_done, 1)

            def exp(j, u):
                hh = u // NT
                w = tiles_of(u % NT)[1] * P
                act.wait_ge(neg_done, j * UNITS + u + 1)
                act.activation(prob[u % 3][:, :w], prob[u % 3][:, :w], ACT.Exp, bias=neg[:, u:u + 1],
                               accum_out=total[:, u:u + 1]).then_inc(exped, 1)
                if with_sink:
                    act.wait_ge(const_in, CONSTS)
                    act.activation(sink_p[:, u:u + 1], sink[:, ds(head_of(j, hh), 1)], ACT.Exp,
                                   bias=neg[:, u:u + 1]).then_inc(sink_done, 1)

            def pt(j, u):
                w = tiles_of(u % NT)[1] * P
                act.wait_ge(transposed, j * UNITS + u + 1)
                act.wait_ge(valued, j * UNITS + u + 1)
                act.activation(pt_hi[u % 2][:, :w], pt_ps[:, :w], ACT.Copy).then_inc(pt_hi_done, 1)

            split_k(0, 0)
            split_q(0, 0)
            split_v(0, 0)
            if shared_kv:
                split_k(1, 1)
                split_v(1, 1)
            with act.Fori(0, NPAIR) as j:
                exp(j, 0)
                for u in range(UNITS):
                    if u + 1 < UNITS:
                        exp(j, u + 1)
                    pt(j, u)
                    if u % NT == 4:
                        h, hh = j * 2 + u // NT + 1, 1 - u // NT
                        act.wait_ge(valued, (h - 1) * NT + 2)
                        split_q(h, hh)
                        if not shared_kv:
                            split_k(h, hh)
                    if u % NT == 6 and not shared_kv:
                        split_v(j * 2 + u // NT + 1, 1 - u // NT)

        @block.vector
        def _(dve):
            def split_q(h, hh):
                dve.wait_ge(q_hi_done, h + 1)
                dve.scalar_tensor_tensor(q_lo[hh][:], q_raw[:], 0.125, q_hi[hh][:],
                                         ALU.mult, ALU.subtract).then_inc(q_lo_done, 1)

            def split_k(h, hh):
                dve.wait_ge(k_hi_done, h + 1)
                dve.tensor_tensor(k_st[hh][DH:P, :], k_raw[DH:P, :], k_st[hh][DH:P, :],
                                  ALU.subtract).then_inc(k_lo_done, 1)

            def split_v(h, hh):
                dve.wait_ge(v_hi_done, h + 1)
                dve.tensor_tensor(v_st[hh][:, :, 1, :], v_ps, v_st[hh][:, :, 0, :],
                                  ALU.subtract).then_inc(v_lo_done, 1)

            def biased(j, u):
                hh = u // NT
                m = tiles_of(u % NT)[1]
                w, skip = m * P, (key_tiles - m) * P
                if u % NT == 0 and not shared_kv:
                    dve.wait_ge(q_in, (j * 2 + hh + 1) * 48)
                dve.wait_ge(scored, j * UNITS + u + 1)
                dve.wait_ge(transposed, j * UNITS + max(u - 2, 0))
                hold(dve, held)
                dve.tensor_tensor_reduce(prob[u % 3][:, :w], s_ps[u % 2][:, :w], bias_sb[hh][:, skip:], 1.0, -3e38,
                                         ALU.add, ALU.max, top[:, u:u + 1]).then_inc(maxed, 1)
                dve.wait_ge(maxed, j * UNITS + u + 3)
                if with_sink:
                    dve.wait_ge(const_in, CONSTS)
                floor = sink[:, ds(head_of(j, hh), 1)] if with_sink else -3e38
                dve.tensor_scalar(neg[:, u:u + 1], top[:, u:u + 1], floor, -1.0,
                                  ALU.max, ALU.mult).then_inc(neg_done, 1)

            def pt(j, u):
                w = tiles_of(u % NT)[1] * P
                dve.wait_ge(pt_hi_done, j * UNITS + u + 1)
                dve.tensor_tensor(pt_lo[u % 2][:, :w], pt_ps[:, :w], pt_hi[u % 2][:, :w],
                                  ALU.subtract).then_inc(pt_lo_done, 1)

            def normalise(j, u):
                hh, n = u // NT, u % NT
                dve.wait_ge(exped, j * UNITS + u + 1)
                if with_sink:
                    dve.wait_ge(sink_done, j * UNITS + u + 1)
                    dve.tensor_tensor(full[:, u:u + 1], total[:, u:u + 1], sink_p[:, u:u + 1],
                                      ALU.add).then_inc(full_done, 1)
                    dve.wait_ge(full_done, j * UNITS + u + 1)
                dve.reciprocal(inv[:, u:u + 1], (full if with_sink else total)[:, u:u + 1]).then_inc(inv_done, 1)
                dve.wait_ge(inv_done, j * UNITS + u + 1)
                dve.wait_ge(valued, j * UNITS + u + 3)
                if n == 0:
                    dve.wait_ge(att_out[hh], j * 16)
                dve.tensor_scalar(o_head[hh][:, n, :], o_ps[u % 2][:, :DH], inv[:, u:u + 1], None,
                                  ALU.mult).then_inc(o_done, 1)

            split_k(0, 0)
            split_q(0, 0)
            split_v(0, 0)
            if shared_kv:
                split_k(1, 1)
                split_v(1, 1)
            with dve.Fori(0, NPAIR) as j:
                biased(j, 0)
                biased(j, 1)
                for u in range(UNITS):
                    if u + 2 < UNITS:
                        biased(j, u + 2)
                    pt(j, u)
                    if u > 0:
                        normalise(j, u - 1)
                    if u % NT == 4:
                        split_q(j * 2 + u // NT + 1, 1 - u // NT)
                        if not shared_kv:
                            split_k(j * 2 + u // NT + 1, 1 - u // NT)
                    if u % NT == 6 and not shared_kv:
                        split_v(j * 2 + u // NT + 1, 1 - u // NT)
                normalise(j, UNITS - 1)

        @block.tensor
        def _(pe):
            pe.sem_inc(maxed, 2)
            pe.sem_inc(valued, 2)
            pe.sem_inc(o_done, 2)

            def turn_v(h, hh):
                pe.wait_ge(kv_in, (h + 1) * 48)
                hold(pe, held)
                for n in range(NT):
                    last = pe.transpose(v_ps[:, n, :], v_raw[:, n * P:(n + 1) * P], idt[:DH, :DH])
                last.then_inc(v_tr, 1)

            def scores(j, u):
                hh, n = u // NT, u % NT
                first, m = tiles_of(n)
                if n == 0:
                    pe.wait_ge(q_lo_done, j * 2 + hh + 1)
                    if shared_kv:
                        pe.wait_ge(k_lo_done, 2)
                    else:
                        pe.wait_ge(k_lo_done, j * 2 + hh + 1)
                pe.wait_ge(maxed, j * UNITS + u + 1)
                for c in range(0, m * P, NB):
                    w = min(NB, m * P - c)
                    keys = k_st[hh][:, first * P + c:first * P + c + w]
                    pe.matmul(s_ps[u % 2][:, c:c + w], q_hi[hh][:, n * P:(n + 1) * P], keys, start=True, stop=False)
                    last = pe.matmul(s_ps[u % 2][:, c:c + w], q_lo[hh][:, n * P:(n + 1) * P], keys,
                                     start=False, stop=True)
                last.then_inc(scored, 1)

            def turn_p(j, u):
                m = tiles_of(u % NT)[1]
                pe.wait_ge(exped, j * UNITS + u + 1)
                pe.wait_ge(pt_lo_done, j * UNITS + u)
                if shared_kv:
                    pe.wait_ge(v_lo_done, 2)
                elif u % NT == 7 or u == 0:
                    pe.wait_ge(v_lo_done, j * 2 + (u + NT - 7) // NT + 1)
                for i in range(m):
                    last = pe.transpose(pt_ps[:, i * P:(i + 1) * P], prob[u % 3][:, i * P:(i + 1) * P], idt[:])
                last.then_inc(transposed, 1)

            def values(j, u):
                hh = u // NT
                first, m = tiles_of(u % NT)
                if u % NT == 0:
                    if shared_kv:
                        pe.wait_ge(v_lo_done, 2)
                    else:
                        pe.wait_ge(v_lo_done, j * 2 + hh + 1)
                pe.wait_ge(pt_lo_done, j * UNITS + u + 1)
                pe.wait_ge(o_done, j * UNITS + u + 1)
                o = o_ps[u % 2][:, :DH]
                for i in range(m):
                    cols = slice(i * P, (i + 1) * P)
                    pe.matmul(o, pt_hi[u % 2][:, cols], v_st[hh][:, first + i, 0, :], start=(i == 0), stop=False)
                    pe.matmul(o, pt_hi[u % 2][:, cols], v_st[hh][:, first + i, 1, :], start=False, stop=False)
                    last = pe.matmul(o, pt_lo[u % 2][:, cols], v_st[hh][:, first + i, 0, :],
                                     start=False, stop=(i == m - 1))
                last.then_inc(valued, 1)

            pe.wait_ge(const_in, CONSTS)
            turn_v(0, 0)
            if shared_kv:
                pe.wait_ge(v_lo_done, 1)
                turn_v(1, 1)
            with pe.Fori(0, NPAIR) as j:
                scores(j, 0)
                scores(j, 1)
                scores(j, 2)
                for u in range(UNITS):
                    turn_p(j, u)
                    if u > 0:
                        values(j, u - 1)
                    if u + 3 < UNITS:
                        scores(j, u + 3)
                    if u % NT == 6 and not shared_kv:
                        pe.wait_ge(pt_lo_done, j * UNITS + u + 1)
                        turn_v(j * 2 + u // NT + 1, 1 - u // NT)
                values(j, UNITS - 1)


def attend_b(nc, feat, band, ident, att, blank):
    rows = lambda tile: lambda j, hh: feat[ds(j * P + (tile * P + hh * DH), DH), :]
    attend(nc, "b", rows(0), rows(4), rows(8), lambda j, hh: j * 2 + hh, False, 5,
           lambda j, hh: band[ds((j * 2 + hh) * P, P), :], None, ident, att, A_COLS, blank)


def attend_a(nc, feat, rotated, mask, sinks, ident, att):
    attend(nc, "a", lambda j, hh: rotated[ds(j * DH + 4 * DH * hh, DH), :],
           lambda j, hh: rotated[(4 * P + hh * DH):(4 * P + hh * DH) + DH, :],
           lambda j, hh: feat[(17 * P + hh * DH):(17 * P + hh * DH) + DH, :],
           lambda j, hh: j + 4 * hh, True, 2, lambda j, hh: mask, sinks, ident, att, 0)


MB = 256
OUT_SLABS = 16


def merge(nc, x, att, gates, w_mix, norm_ffn, ident, x2, h2):
    with Stage(nc, "mg") as st:
        w_hi = st.sb("w_hi", [P, OUT_SLABS, D], F32R)
        w_lo = st.sb("w_lo", [P, OUT_SLABS, D], F32R)
        w_raw = [st.sb(f"w_raw{p}", [P, D]) for p in range(2)]
        att_in = w_raw
        aT_hi = st.sb("aT_hi", [P, KD, MB], F32R)
        aT_lo = st.sb("aT_lo", [P, KD, MB], F32R)
        mix_hi = st.sb("mix_hi", [P, KD, MB], F32R)
        mix_lo = st.sb("mix_lo", [P, KD, MB], F32R)
        g_in = [st.sb(f"g_in{p}", [P, 2 * MB]) for p in range(2)]
        gated = [st.sb(f"gated{p}", [P, 2 * MB]) for p in range(2)]
        mixed = [st.sb(f"mixed{p}", [P, MB]) for p in range(2)]
        x_t = [st.sb(f"x_t{p}", [P, D]) for p in range(2)]
        h_t = st.sb("h_t", [P, D])
        junk = st.sb("junk", [P, D], BF16)
        g_row = st.sb("g_row", [P, D])
        idt = st.sb("idt", [P, P])
        stat = [st.sb(f"stat{p}", [P, 8]) for p in range(2)]
        t_ps = [st.ps(f"t_ps{b}", [P, NB]) for b in range(2)]
        y_ps = [st.ps(f"y_ps{b}", [P, 2, MB]) for b in range(2)]
        o_ps = [st.ps(f"o_ps{b}", [P, NB]) for b in range(2)]

        held = st.sem("held")
        const_in = st.sem("const_in")
        w_in = [st.sem(f"w_in{p}") for p in range(2)]
        w_hi_done = st.sem("w_hi_done")
        w_lo_done = st.sem("w_lo_done")
        att_ready = [st.sem(f"att_ready{p}") for p in range(2)]
        att_turned = st.sem("att_turned")
        a_hi_done = st.sem("a_hi_done")
        a_lo_done = st.sem("a_lo_done")
        g_ready = [st.sem(f"g_ready{p}") for p in range(2)]
        y_done = st.sem("y_done")
        gated_done = st.sem("gated_done")
        mixed_done = st.sem("mixed_done")
        mix_hi_done = st.sem("mix_hi_done")
        mix_lo_done = st.sem("mix_lo_done")
        out_done = st.sem("out_done")
        x_ready = [st.sem(f"x_ready{p}") for p in range(2)]
        x2_done = st.sem("x2_done")
        ssq_done = st.sem("ssq_done")
        mean_done = st.sem("mean_done")
        root_done = st.sem("root_done")
        rstd_done = st.sem("rstd_done")
        h_done = st.sem("h_done")
        x2_out = [st.sem(f"x2_out{p}") for p in range(2)]
        h_out = st.sem("h_out")
        block = st.block()
        NBLK = SEQ // MB

        @block.sync
        def _(sp):
            sp.dma_start(g_row[:], norm_ffn.partition_broadcast(P)).then_inc(const_in, 16)
            sp.dma_start(idt[:], ident).then_inc(const_in, 16)
            for s in range(OUT_SLABS):
                if s >= 2:
                    sp.wait_ge(w_lo_done, s - 1)
                sp.dma_start(w_raw[s % 2][:], w_mix[s]).then_inc(w_in[s % 2], 16)
            sp.wait_ge(w_lo_done, OUT_SLABS)

            def load_att(i):
                for t in range(2):
                    sp.dma_start(att_in[t][:], att[ds(i * MB + t * P, P), :]).then_inc(att_ready[t], 16)

            load_att(0)
            with sp.Fori(0, NBLK) as i:
                for t in range(2):
                    sp.wait_ge(x2_out[t], i * 16)
                    hold(sp, held)
                    sp.wait_ge(h_done, i * 2 + t + 1)
                    hold(sp, held)
                    sp.dma_start(x_t[t][:], x[ds(i * MB + t * P, P), :]).then_inc(x_ready[t], 16)
                for o in range(KD):
                    sp.wait_ge(gated_done, i * KD + o + 1)
                    hold(sp, held)
                    for br in range(2):
                        sp.dma_start(g_in[o % 2][:, br * MB:(br + 1) * MB],
                                     gates[br * KD + o, :, ds(i * MB, MB)]).then_inc(g_ready[o % 2], 16)
                sp.wait_ge(att_turned, i * 4 + 4)
                hold(sp, held)
                nxt = i * MB + MB
                for t in range(2):
                    sp.dma_start(att_in[t][:], att[ds(nxt + t * P, P), :]).then_inc(att_ready[t], 16)
            for t in range(2):
                sp.wait_ge(x2_out[t], 16 * NBLK)
                sp.wait_ge(att_ready[t], 16 * (NBLK + 1))
            sp.wait_ge(h_out, 16 * NT)

        @block.gpsimd
        def _(pool):
            with pool.Fori(0, NBLK) as i:
                for o in range(KD):
                    pool.wait_ge(gated_done, i * KD + o + 3)
                    pool.wait_ge(mix_lo_done, i * KD + o + 1)
                    pool.tensor_tensor(mixed[o % 2][:], gated[o % 2][:, :MB], gated[o % 2][:, MB:],
                                       ALU.add).then_inc(mixed_done, 1)

        @block.scalar
        def _(act):
            for s in range(OUT_SLABS):
                act.wait_ge(w_in[s % 2], 16 * (s // 2 + 1))
                act.activation(w_hi[:, s, :], w_raw[s % 2][:], ACT.Copy).then_inc(w_hi_done, 1)

            def att_hi(i):
                for t in range(2):
                    for b in range(2):
                        act.wait_ge(att_turned, i * 4 + 2 * t + b + 1)
                        act.activation(aT_hi[:, 4 * b:4 * b + 4, t * P:(t + 1) * P],
                                       t_ps[b][:].rearrange("p (k t) -> p k t", k=4), ACT.Copy).then_inc(a_hi_done, 1)

            att_hi(0)
            with act.Fori(0, NBLK) as i:
                for o in range(KD):
                    act.wait_ge(mixed_done, i * KD + o + 3)
                    if o == 0:
                        act.wait_ge(out_done, i * 2)
                    act.activation(mix_hi[:, o, :], mixed[o % 2][:], ACT.Copy).then_inc(mix_hi_done, 1)
                att_hi(i + 1)
                for t in range(2):
                    act.wait_ge(x2_done, i * 4 + 2 * t + 2)
                    act.wait_ge(ssq_done, i * 2 + t)
                    act.activation(junk[:], x_t[t][:], ACT.Square, accum_out=stat[t][:, 0:1]).then_inc(ssq_done, 1)
                    act.wait_ge(mean_done, i * 2 + t + 1)
                    act.activation(stat[t][:, 2:3], stat[t][:, 1:2], ACT.Sqrt).then_inc(root_done, 1)
                    act.dma_start(x2[ds(i * MB + t * P, P), :], x_t[t][:]).then_inc(x2_out[t], 16)
                    act.wait_ge(h_done, i * 2 + t + 3)
                    act.dma_start(h2[ds(i * MB + t * P, P), :], h_t[:]).then_inc(h_out, 16)

        @block.vector
        def _(dve):
            for s in range(OUT_SLABS):
                dve.wait_ge(w_hi_done, s + 1)
                dve.tensor_tensor(w_lo[:, s, :], w_raw[s % 2][:], w_hi[:, s, :], ALU.subtract).then_inc(w_lo_done, 1)
            dve.wait_ge(const_in, 32)

            def att_lo(i):
                for t in range(2):
                    for b in range(2):
                        dve.wait_ge(a_hi_done, i * 4 + 2 * t + b + 1)
                        where = (slice(None), slice(4 * b, 4 * b + 4), slice(t * P, (t + 1) * P))
                        dve.tensor_tensor(aT_lo[where], t_ps[b][:].rearrange("p (k t) -> p k t", k=4),
                                          aT_hi[where], ALU.subtract).then_inc(a_lo_done, 1)

            def gate(i, o):
                dve.wait_ge(g_ready[o % 2], i * (KD // 2 * 32) + (o // 2 + 1) * 32)
                dve.wait_ge(y_done, i * KD + o + 1)
                dve.wait_ge(mixed_done, i * KD + o + 1)
                dve.tensor_tensor(gated[o % 2][:], y_ps[o % 2][:].rearrange("p a t -> p (a t)"), g_in[o % 2][:],
                                  ALU.mult).then_inc(gated_done, 1)

            att_lo(0)
            with dve.Fori(0, NBLK) as i:
                gate(i, 0)
                for o in range(KD):
                    if o + 1 < KD:
                        gate(i, o + 1)
                    dve.wait_ge(mix_hi_done, i * KD + o + 1)
                    dve.tensor_tensor(mix_lo[:, o, :], mixed[o % 2][:], mix_hi[:, o, :],
                                      ALU.subtract).then_inc(mix_lo_done, 1)
                att_lo(i + 1)
                for t in range(2):
                    dve.wait_ge(x_ready[t], i * 16 + 16)
                    dve.wait_ge(out_done, i * 2 + t + 1)
                    for b in range(2):
                        cols = slice(b * NB, (b + 1) * NB)
                        dve.tensor_tensor(x_t[t][:, cols], o_ps[b][:], x_t[t][:, cols], ALU.add).then_inc(x2_done, 1)
                    rms_tail(dve, stat[t], (i * 2 + t), ssq_done, mean_done, root_done, rstd_done)
                    dve.wait_ge(h_out, (i * 2 + t) * 16)
                    dve.scalar_tensor_tensor(h_t[:], x_t[t][:], stat[t][:, 6:7], g_row[:],
                                             ALU.mult, ALU.mult).then_inc(h_done, 1)

        @block.tensor
        def _(pe):
            pe.sem_inc(a_lo_done, 2)
            pe.sem_inc(gated_done, 2)
            pe.sem_inc(mixed_done, 2)
            pe.sem_inc(mix_lo_done, 2)
            pe.sem_inc(h_done, 2)
            pe.wait_ge(const_in, 32)

            def turn_att(i):
                for t in range(2):
                    pe.wait_ge(att_ready[t], i * 16 + 16)
                    for b in range(2):
                        pe.wait_ge(a_lo_done, i * 4 + 2 * t + b + 1)
                        for k in range(4):
                            last = pe.transpose(t_ps[b][:, k * P:(k + 1) * P],
                                                att_in[t][:, (4 * b + k) * P:(4 * b + k + 1) * P], idt[:])
                        last.then_inc(att_turned, 1)

            turn_att(0)
            with pe.Fori(0, NBLK) as i:
                pe.wait_ge(a_lo_done, i * 4 + 6)
                for o in range(KD):
                    pe.wait_ge(gated_done, i * KD + o + 1)
                    cols = slice(o * P, (o + 1) * P)
                    for br in range(2):
                        for k in range(4 * br, 4 * br + 4):
                            y = y_ps[o % 2][:, br, :]
                            pe.matmul(y, w_hi[:, k, cols], aT_hi[:, k, :], start=(k % 4 == 0), stop=False)
                            pe.matmul(y, w_hi[:, k, cols], aT_lo[:, k, :], start=False, stop=False)
                            last = pe.matmul(y, w_lo[:, k, cols], aT_hi[:, k, :], start=False, stop=(k % 4 == 3))
                    last.then_inc(y_done, 1)
                turn_att(i + 1)
                pe.wait_ge(mix_lo_done, i * KD + KD + 2)
                for t in range(2):
                    pe.wait_ge(x2_done, i * 4 + 2 * t)
                    tok = slice(t * P, (t + 1) * P)
                    for k in range(KD):
                        for m, w, first, end in ((mix_hi, w_hi, k == 0, False), (mix_hi, w_lo, False, False),
                                                 (mix_lo, w_hi, False, k == KD - 1)):
                            for b in range(2):
                                last = pe.matmul(o_ps[b][:], m[:, k, tok], w[:, KD + k, b * NB:(b + 1) * NB],
                                                 start=first, stop=end)
                    last.then_inc(out_done, 1)


GROUPS = 4
PER_GROUP = 8
EXPERTS = GROUPS * PER_GROUP
LOGITS = GROUPS + EXPERTS
MAX_TILES = 2 * SEQ // P + EXPERTS
BIG = 3e38


class Routes:

    def __init__(self, st):
        self.slot = [st.sb(f"slot{k}", [P, NT], U32) for k in range(2)]
        self.weight = [st.sb(f"weight{k}", [P, NT]) for k in range(2)]
        self.token = st.sb("token", [P, MAX_TILES + 2], U32)
        self.first = st.sb("first", [1, EXPERTS], I32)
        self.last = st.sb("last", [1, EXPERTS], I32)


def route(nc, h2, w_router, b_router, ident, strict_upper, token_ids, table, routes):
    with Stage(nc, "rt") as st:
        h_in = [st.sb(f"h_in{p}", [P, D]) for p in range(2)]
        hT = [st.sb(f"hT{p}", [P, KD, P]) for p in range(2)]
        w_r = st.sb("w_r", [P, KD, LOGITS])
        b_r = st.sb("b_r", [P, LOGITS])
        idt = st.sb("idt", [P, P])
        upper = st.sb("upper", [P, P])
        ones = st.sb("ones", [P, P])
        ids = st.sb("ids", [P, NT])
        logit = st.sb("logit", [P, NT, LOGITS])
        t_ps = [[st.ps(f"t_ps{p}{b}", [P, NB]) for b in range(2)] for p in range(2)]
        l_ps = [st.ps(f"l_ps{p}", [P, NB]) for p in range(2)]
        c_ps = [st.ps(f"c_ps{b}", [P, NT, EXPERTS]) for b in range(2)]

        held = st.sem("held")
        const_in = st.sem("const_in")
        h_ready = [st.sem(f"h_ready{p}") for p in range(2)]
        turned = st.sem("turned")
        copied = st.sem("copied")
        logit_mm = st.sem("logit_mm")
        logit_done = st.sem("logit_done")
        exp_asked = st.sem("exp_asked")
        exp_done = st.sem("exp_done")
        count_asked = st.sem("count_asked")
        counted = st.sem("counted")
        routed = st.sem("routed")
        zeroed = st.sem("zeroed")
        scattered = st.sem("scattered")
        table_in = st.sem("table_in")
        table_turned = st.sem("table_turned")
        step = st.sem("step")
        block = st.block()

        g4 = st.sb("g4", [P, NT, GROUPS])
        g_hot = st.sb("g_hot", [P, NT, GROUPS])
        g_work = st.sb("g_work", [P, NT, GROUPS])
        g_exp = st.sb("g_exp", [P, NT, GROUPS])
        prio4 = st.sb("prio4", [P, NT, GROUPS])
        prio8 = st.sb("prio8", [P, NT, PER_GROUP])
        wide = st.sb("wide", [P, NT, GROUPS, PER_GROUP])
        inner = st.sb("inner", [P, NT, PER_GROUP])
        inner2 = st.sb("inner2", [P, NT, PER_GROUP])
        e8 = st.sb("e8", [P, NT, PER_GROUP])
        hot8 = [st.sb(f"hot8{k}", [P, NT, PER_GROUP]) for k in range(2)]
        hot = [st.sb(f"hot{k}", [P, NT, EXPERTS]) for k in range(2)]
        both = st.sb("both", [P, NT, EXPERTS])
        rank = st.sb("rank", [P, NT, EXPERTS])
        base = st.sb("base", [P, NT + 1, EXPERTS])
        picked = st.sb("picked", [P, NT, EXPERTS])
        top = st.sb("top", [P, 8, NT])
        slot_f = st.sb("slot_f", [P, 2, NT])
        place = [st.sb(f"place{k}", [P, NT], U32) for k in range(2)]
        cnt_i = st.sb("cnt_i", [P, EXPERTS], I32)
        tiles_f = st.sb("tiles_f", [P, EXPERTS])
        ends = st.sb("ends", [P, EXPERTS])
        starts = st.sb("starts", [P, EXPERTS])
        one_row = st.sb("one_row", [P, EXPERTS])
        zero = st.sb("zero", [MAX_TILES, P])
        tab = st.sb("tab", [MAX_TILES, P])

        @block.sync
        def _(sp):
            sp.dma_start(w_r[:], w_router.rearrange("p (k n) -> p k n", k=KD)).then_inc(const_in, 16)
            sp.dma_start(b_r[:], b_router.partition_broadcast(P)).then_inc(const_in, 16)
            sp.dma_start(idt[:], ident).then_inc(const_in, 16)
            sp.dma_start(upper[:], strict_upper).then_inc(const_in, 16)
            sp.dma_start(ids[:], token_ids).then_inc(const_in, 16)
            for p in range(2):
                sp.dma_start(h_in[p][:], h2[p * P:(p + 1) * P, :]).then_inc(h_ready[p], 16)
            with sp.Fori(1, NT // 2) as i:
                for p in range(2):
                    sp.wait_ge(turned, i * 2 + p - 1)
                    hold(sp, held)
                    sp.dma_start(h_in[p][:], h2[ds((i * 2 + p) * P, P), :]).then_inc(h_ready[p], 16)

        @block.gpsimd
        def _(pool):
            pool.memset(zero[:], 0.0).then_inc(zeroed, 1)
            pool.memset(ones[:], 1.0).then_inc(zeroed, 1)
            pool.wait_ge(zeroed, 2)
            pool.dma_start(table.rearrange("(t p) a -> t (p a)", p=P), zero[:]).then_inc(scattered, 16)
            pool.wait_ge(scattered, 16)
            pool.wait_ge(const_in, 80)
            pool.wait_ge(routed, 1)
            for t in range(NT):
                for k in range(2):
                    pool.indirect_dma_start(
                        out=table, out_offset=bass.IndirectOffsetOnAxis(ap=place[k][:, t:t + 1], axis=0),
                        in_=ids[:, t:t + 1], in_offset=None).then_inc(scattered, 16)
            pool.wait_ge(scattered, 16 * (2 * NT + 1))
            pool.dma_start(tab[:], table.rearrange("(t p) a -> t (p a)", p=P)).then_inc(table_in, 16)

        @block.scalar
        def _(act):
            with act.Fori(0, NT // 2) as i:
                for p in range(2):
                    act.wait_ge(turned, i * 2 + p + 1)
                    for b in range(2):
                        act.activation(hT[p][:, 4 * b:4 * b + 4, :], t_ps[p][b][:].rearrange("p (k t) -> p k t", k=4),
                                       ACT.Copy).then_inc(copied, 1)
            act.wait_ge(exp_asked, 1)
            act.activation(g_exp[:], g4[:], ACT.Exp).then_inc(exp_done, 1)
            act.wait_ge(exp_asked, 2)
            act.activation(top[:, 4, :], top[:, 3, :], ACT.Exp).then_inc(exp_done, 1)

        @block.tensor
        def _(pe):
            pe.wait_ge(const_in, 80)
            with pe.Fori(0, NT // 2) as i:
                for p in range(2):
                    pe.wait_ge(h_ready[p], i * 16 + 16)
                    for k in range(KD):
                        last = pe.transpose(t_ps[p][k // 4][:, (k % 4) * P:(k % 4 + 1) * P],
                                            h_in[p][:, k * P:(k + 1) * P], idt[:])
                    last.then_inc(turned, 1)
                for p in range(2):
                    pe.wait_ge(copied, i * 4 + 2 * p + 2)
                    pe.wait_ge(logit_done, i * 2)
                    for k in range(KD):
                        last = pe.matmul(l_ps[p][:, :LOGITS], hT[p][:, k, :], w_r[:, k, :],
                                         start=(k == 0), stop=(k == KD - 1))
                    last.then_inc(logit_mm, 1)
            pe.wait_ge(count_asked, 1)
            flat = both[:].rearrange("p t e -> p (t e)")
            pe.matmul(c_ps[0][:].rearrange("p t e -> p (t e)"), upper[:], flat, start=True, stop=True)
            pe.wait_ge(zeroed, 2)
            pe.matmul(c_ps[1][:].rearrange("p t e -> p (t e)"), ones[:], flat,
                      start=True, stop=True).then_inc(counted, 1)
            pe.wait_ge(table_in, 16)
            pe.transpose(l_ps[0][:, :MAX_TILES], tab[:], idt[:MAX_TILES, :MAX_TILES]).then_inc(table_turned, 1)

        @block.vector
        def _(dve):
            n = [0]

            def then(ins, sem=None):
                n[0] += 1
                ins.then_inc(step, 1)
                dve.wait_ge(step, n[0])

            def over(ap, m):
                return ap.unsqueeze(2).broadcast_to([P, NT, m])

            dve.wait_ge(const_in, 80)
            with dve.Fori(0, NT // 2) as i:
                for p in range(2):
                    dve.wait_ge(logit_mm, i * 2 + p + 1)
                    hold(dve, held)
                    dve.tensor_tensor(logit[:, ds(i * 2 + p, 1), :].rearrange("p a n -> p (a n)"),
                                      l_ps[p][:, :LOGITS], b_r[:], ALU.add).then_inc(logit_done, 1)
            for g in range(GROUPS):
                then(dve.memset(prio4[:, :, g], float(GROUPS - g)))
            for e in range(PER_GROUP):
                then(dve.memset(prio8[:, :, e], float(PER_GROUP - e)))
            then(dve.memset(one_row[:], 1.0))
            dve.wait_ge(logit_done, NT)
            g_logit = logit[:, :, :GROUPS]
            e_logit = logit[:, :, GROUPS:].rearrange("p t (g e) -> p t g e", g=GROUPS)

            def first_of(hot_out, value, high, prio, work, slot):
                m = value.shape[2]
                then(dve.tensor_tensor(work, value, over(high, m), ALU.is_equal))
                then(dve.tensor_tensor(work, work, prio, ALU.mult))
                then(dve.tensor_reduce(top[:, slot, :], work, AX_X, ALU.max))
                then(dve.tensor_tensor(hot_out, work, over(top[:, slot, :], m), ALU.is_equal))

            then(dve.tensor_reduce(top[:, 0, :], g_logit, AX_X, ALU.max))
            dve.tensor_tensor(g4[:], g_logit, over(top[:, 0, :], GROUPS), ALU.subtract).then_inc(exp_asked, 1)
            first_of(g_hot[:], g_logit, top[:, 0, :], prio4[:], g_work[:], 5)
            then(dve.tensor_tensor(wide[:], e_logit,
                                   g_hot[:].unsqueeze(3).broadcast_to([P, NT, GROUPS, PER_GROUP]), ALU.mult))
            then(dve.tensor_reduce(inner[:], wide[:].rearrange("p t g e -> p t e g"), AX_X, ALU.add))
            then(dve.tensor_reduce(top[:, 1, :], inner[:], AX_X, ALU.max))
            first_of(hot8[0][:], inner[:], top[:, 1, :], prio8[:], e8[:], 5)
            then(dve.scalar_tensor_tensor(inner2[:], hot8[0][:], -BIG, inner[:], ALU.mult, ALU.add))
            then(dve.tensor_reduce(top[:, 2, :], inner2[:], AX_X, ALU.max))
            first_of(hot8[1][:], inner2[:], top[:, 2, :], prio8[:], e8[:], 5)
            then(dve.tensor_tensor(top[:, 3, :], top[:, 2, :], top[:, 1, :], ALU.subtract))
            dve.sem_inc(exp_asked, 1)
            for k in range(2):
                then(dve.tensor_tensor(hot[k][:].rearrange("p t (g e) -> p t g e", g=GROUPS),
                                       g_hot[:].unsqueeze(3).broadcast_to([P, NT, GROUPS, PER_GROUP]),
                                       hot8[k][:].unsqueeze(2).broadcast_to([P, NT, GROUPS, PER_GROUP]), ALU.mult))
            dve.tensor_tensor(both[:], hot[0][:], hot[1][:], ALU.add).then_inc(count_asked, 1)
            dve.wait_ge(exp_done, 2)
            then(dve.tensor_reduce(top[:, 5, :], g_exp[:], AX_X, ALU.add))
            then(dve.scalar_tensor_tensor(top[:, 6, :], top[:, 4, :], 1.0, top[:, 5, :], ALU.add, ALU.mult))
            then(dve.reciprocal(routes.weight[0][:], top[:, 6, :]))
            then(dve.tensor_tensor(routes.weight[1][:], routes.weight[0][:], top[:, 4, :], ALU.mult))
            dve.wait_ge(counted, 1)
            then(dve.memset(base[:, 0, :], 0.0))
            for t in range(NT):
                then(dve.tensor_tensor(base[:, t + 1, :], c_ps[1][:, t, :], base[:, t, :], ALU.add))
            then(dve.tensor_tensor(rank[:], c_ps[0][:], base[:, :NT, :], ALU.add))
            then(dve.tensor_scalar(cnt_i[:], base[:, NT, :], float(P - 1), None, ALU.add))
            then(dve.tensor_single_scalar(cnt_i[:], cnt_i[:], 7, ALU.arith_shift_right))
            then(dve.tensor_scalar(tiles_f[:], cnt_i[:], 1.0, None, ALU.max))
            then(dve.tensor_tensor_scan(ends[:], one_row[:], tiles_f[:], 0.0, ALU.mult, ALU.add))
            then(dve.tensor_tensor(starts[:], ends[:], tiles_f[:], ALU.subtract))
            then(dve.tensor_copy(routes.first[:], starts[0:1, :]))
            then(dve.tensor_scalar(routes.last[:], ends[0:1, :], -1.0, None, ALU.add))
            then(dve.tensor_scalar(starts[:], starts[:], float(P), None, ALU.mult))
            then(dve.tensor_tensor(rank[:], rank[:],
                                   starts[:].unsqueeze(1).broadcast_to([P, NT, EXPERTS]), ALU.add))
            for k in range(2):
                then(dve.tensor_tensor(picked[:], rank[:], hot[k][:], ALU.mult))
                then(dve.tensor_reduce(slot_f[:, k, :], picked[:], AX_X, ALU.add))
                then(dve.tensor_copy(place[k][:], slot_f[:, k, :]))
                then(dve.tensor_scalar(routes.slot[k][:], slot_f[:, k, :], float(P), None, ALU.add))
            dve.sem_inc(routed, 1)
            dve.wait_ge(table_turned, 1)
            then(dve.memset(routes.token[:, MAX_TILES:], 0))
            then(dve.tensor_copy(routes.token[:, :MAX_TILES], l_ps[0][:, :MAX_TILES]))


DE = 512
KE = DE // P
CHUNKS = 4


def experts(nc, h2, w_gate, w_up, w_down, ident, ys, routes):
    with Stage(nc, "ex") as st:
        raw = [[st.sb(f"raw_{m}{j}", [P, D]) for j in range(CHUNKS)] for m in "gud"]
        wg_hi, wg_lo, wu_hi, wu_lo = (st.sb(n, [P, KD, DE], F32R) for n in ("wg_hi", "wg_lo", "wu_hi", "wu_lo"))
        wd_hi = [st.sb(f"wd_hi{p}", [P, KE, D], F32R) for p in range(2)]
        wd_lo = [st.sb(f"wd_lo{p}", [P, KE, D], F32R) for p in range(2)]
        idt = st.sb("idt", [P, P])
        rows = st.sb("rows", [P, 1], U32)
        x_in = st.sb("x_in", [P, D])
        xT_hi, xT_lo = st.sb("xT_hi", [P, KD, P], F32R), st.sb("xT_lo", [P, KD, P], F32R)
        silu = st.sb("silu", [P, DE])
        a = st.sb("a", [P, DE])
        aT_hi, aT_lo = st.sb("aT_hi", [P, KE, P], F32R), st.sb("aT_lo", [P, KE, P], F32R)
        y = st.sb("y", [P, D])
        g_ps, u_ps, a_ps = (st.ps(n, [P, NB]) for n in ("g_ps", "u_ps", "a_ps"))
        x_ps = [st.ps(f"x_ps{b}", [P, NB]) for b in range(2)]
        y_ps = [st.ps(f"y_ps{b}", [P, NB]) for b in range(2)]

        held = st.sem("held")
        idt_in = st.sem("idt_in")
        raw_in = [[st.sem(f"raw_in_{m}{j}") for j in range(CHUNKS)] for m in "gud"]
        g_hi_done, u_hi_done, d_hi_done = (st.sem(n) for n in ("g_hi_done", "u_hi_done", "d_hi_done"))
        g_lo_done, u_lo_done, d_lo_done = (st.sem(n) for n in ("g_lo_done", "u_lo_done", "d_lo_done"))
        rows_ready = st.sem("rows_ready")
        x_ready = st.sem("x_ready")
        x_turned = st.sem("x_turned")
        xT_hi_done, xT_lo_done = st.sem("xT_hi_done"), st.sem("xT_lo_done")
        gate_done, up_done = st.sem("gate_done"), st.sem("up_done")
        silu_done = st.sem("silu_done")
        a_done = st.sem("a_done")
        a_turned = st.sem("a_turned")
        aT_hi_done, aT_lo_done = st.sem("aT_hi_done"), st.sem("aT_lo_done")
        down_done = st.sem("down_done")
        y_done = st.sem("y_done")
        y_stored = st.sem("y_stored")
        block = st.block()

        def slabs(buffer, m, j):
            return buffer[:, 2 * j:2 * j + 2, :].rearrange("p k n -> p (k n)") if m < 2 else buffer[:, j, :]

        def span(eng, e):
            first = eng.value_load(routes.first[0:1, ds(e, 1)], min_val=0, max_val=MAX_TILES - 1)
            last = eng.value_load(routes.last[0:1, ds(e, 1)], min_val=0, max_val=MAX_TILES - 1)
            return first, last

        def last_of_all(eng):
            return eng.value_load(routes.last[0:1, EXPERTS - 1:EXPERTS], min_val=0, max_val=MAX_TILES - 1)

        def over_experts(eng, each):
            with eng.Fori(0, EXPERTS // 2 - 1) as i:
                for p in range(2):
                    each(i * 2 + p, p, True)
            each(EXPERTS - 2, 0, True)
            each(EXPERTS - 1, 1, False)

        @block.sync
        def _(sp):
            def load(e, m, j):
                if m < 2:
                    sp.dma_start(raw[m][j][:].rearrange("p (s n) -> p s n", s=2),
                                 (w_gate, w_up)[m][ds(e, 1), 2 * j * P:(2 * j + 2) * P, :].rearrange(
                                     "a (s p) n -> p (a s) n", p=P)).then_inc(raw_in[m][j], 16)
                else:
                    sp.dma_start(raw[m][j][:], w_down[ds(e, 1), j * P:(j + 1) * P, :].rearrange(
                        "a p n -> (a p) n")).then_inc(raw_in[m][j], 16)

            sp.dma_start(idt[:], ident).then_inc(idt_in, 16)
            for m in range(3):
                for j in range(CHUNKS):
                    load(0, m, j)
            with sp.Fori(1, EXPERTS) as e:
                for m in range(3):
                    for j in range(CHUNKS):
                        sp.wait_ge((g_lo_done, u_lo_done, d_lo_done)[m], e * CHUNKS + (j + 1 - CHUNKS))
                        hold(sp, held)
                        load(e, m, j)

        @block.gpsimd
        def _(pool):
            def gather(n):
                pool.tensor_copy(rows[:], routes.token[:, ds(n, 1)]).then_inc(rows_ready, 1)
                pool.wait_ge(rows_ready, n + 1)
                hold(pool, held)
                pool.indirect_dma_start(out=x_in[:], out_offset=None, in_=h2,
                                        in_offset=bass.IndirectOffsetOnAxis(ap=rows[:, 0:1], axis=0)
                                        ).then_inc(x_ready, 16)

            def step(n):
                pool.wait_ge(x_turned, n + 2)
                gather(n + 2)
                pool.wait_ge(y_done, n + 1)
                hold(pool, held)
                pool.dma_start(ys[ds(n * P, P), :], y[:]).then_inc(y_stored, 16)

            def split_down(e, p):
                for j in range(CHUNKS):
                    pool.wait_ge(d_hi_done, e * CHUNKS + j + 1)
                    pool.tensor_tensor(wd_lo[p][:, j, :], raw[2][j][:], wd_hi[p][:, j, :],
                                       ALU.subtract).then_inc(d_lo_done, 1)

            gather(0)
            pool.wait_ge(x_turned, 1)
            gather(1)
            split_down(0, 0)

            def each(e, p, more):
                first, last = span(pool, e)
                with pool.Fori(first, last + 1) as n:
                    step(n)
                if more:
                    split_down(e + 1, 1 - p)

            over_experts(pool, each)
            end = last_of_all(pool) + 1
            pool.wait_ge(y_done, end + 1)
            hold(pool, held)
            pool.dma_start(ys[ds(end * P, P), :], y[:]).then_inc(y_stored, 16)
            pool.wait_ge(y_stored, end * 16 + 16)
            pool.wait_ge(x_ready, end * 16 + 32)

        @block.scalar
        def _(act):
            def split(e, m, dst, done):
                for j in range(CHUNKS):
                    act.wait_ge(raw_in[m][j], e * 16 + 16)
                    act.activation(slabs(dst, m, j), raw[m][j][:], ACT.Copy).then_inc(done, 1)

            def silu_and_aT(n):
                act.wait_ge(gate_done, n + 1)
                act.wait_ge(a_done, n + 1)
                act.activation(silu[:], g_ps[:], ACT.Silu).then_inc(silu_done, 1)
                act.wait_ge(a_turned, n + 1)
                act.activation(aT_hi[:].rearrange("p k t -> p (k t)"), a_ps[:], ACT.Copy).then_inc(aT_hi_done, 1)

            def xT(n):
                act.wait_ge(x_turned, n + 1)
                for b in range(2):
                    act.activation(xT_hi[:, 4 * b:4 * b + 4, :], x_ps[b][:].rearrange("p (k t) -> p k t", k=4),
                                   ACT.Copy).then_inc(xT_hi_done, 1)

            split(0, 0, wg_hi, g_hi_done)
            xT(0)
            split(0, 1, wu_hi, u_hi_done)
            split(0, 2, wd_hi[0], d_hi_done)

            def each(e, p, more):
                first, last = span(act, e)
                with act.If(last > first):
                    with act.Fori(first, last) as n:
                        silu_and_aT(n)
                        xT(n + 1)
                silu_and_aT(last)
                if more:
                    split(e + 1, 0, wg_hi, g_hi_done)
                xT(last + 1)
                if more:
                    split(e + 1, 1, wu_hi, u_hi_done)
                    act.wait_ge(down_done, first + 1)
                    split(e + 1, 2, wd_hi[1 - p], d_hi_done)

            over_experts(act, each)
            end = last_of_all(act) + 1
            act.wait_ge(a_turned, end + 1)
            act.activation(aT_hi[:].rearrange("p k t -> p (k t)"), a_ps[:], ACT.Copy).then_inc(aT_hi_done, 1)

        @block.vector
        def _(dve):
            def split(e, m, hi, lo, hi_done, lo_done):
                for j in range(CHUNKS):
                    dve.wait_ge(hi_done, e * CHUNKS + j + 1)
                    dve.tensor_tensor(slabs(lo, m, j), raw[m][j][:], slabs(hi, m, j),
                                      ALU.subtract).then_inc(lo_done, 1)

            def aT(n):
                dve.wait_ge(aT_hi_done, n + 1)
                dve.tensor_tensor(aT_lo[:].rearrange("p k t -> p (k t)"), a_ps[:],
                                  aT_hi[:].rearrange("p k t -> p (k t)"), ALU.subtract).then_inc(aT_lo_done, 1)

            def a_and_xT(n):
                dve.wait_ge(up_done, n + 1)
                dve.wait_ge(silu_done, n + 1)
                dve.tensor_tensor(a[:], u_ps[:], silu[:], ALU.mult).then_inc(a_done, 1)
                xT(n + 1)

            def xT(n):
                for b in range(2):
                    dve.wait_ge(xT_hi_done, n * 2 + b + 1)
                    dve.tensor_tensor(xT_lo[:, 4 * b:4 * b + 4, :], x_ps[b][:].rearrange("p (k t) -> p k t", k=4),
                                      xT_hi[:, 4 * b:4 * b + 4, :], ALU.subtract).then_inc(xT_lo_done, 1)

            def y_out(n):
                dve.wait_ge(down_done, n + 1)
                dve.wait_ge(y_stored, n * 16)
                dve.tensor_copy(y[:, :NB], y_ps[0][:])
                dve.tensor_copy(y[:, NB:], y_ps[1][:]).then_inc(y_done, 1)

            dve.memset(a[:], 0.0).then_inc(a_done, 1)
            split(0, 0, wg_hi, wg_lo, g_hi_done, g_lo_done)
            xT(0)
            split(0, 1, wu_hi, wu_lo, u_hi_done, u_lo_done)

            def each(e, p, more):
                first, last = span(dve, e)
                with dve.If(last > first):
                    with dve.Fori(first, last) as n:
                        aT(n)
                        a_and_xT(n)
                        y_out(n)
                aT(last)
                if more:
                    split(e + 1, 0, wg_hi, wg_lo, g_hi_done, g_lo_done)
                a_and_xT(last)
                if more:
                    split(e + 1, 1, wu_hi, wu_lo, u_hi_done, u_lo_done)
                y_out(last)

            over_experts(dve, each)
            end = last_of_all(dve) + 1
            aT(end)
            y_out(end)

        @block.tensor
        def _(pe):
            def times(out, xT_parts, w_parts, chunk, cols):
                for k in chunk:
                    for c, (x, w) in enumerate(((0, 0), (1, 0), (0, 1))):
                        last = pe.matmul(out, xT_parts[x][:, k, :], w_parts[w][:, k, cols],
                                         start=(k == 0 and c == 0), stop=(k == xT_parts[2] - 1 and c == 2))
                return last

            xT = (xT_hi, xT_lo, KD)
            aT = (aT_hi, aT_lo, KE)

            def turn_a():
                for k in range(KE):
                    last = pe.transpose(a_ps[:, k * P:(k + 1) * P], a[:, k * P:(k + 1) * P], idt[:])
                last.then_inc(a_turned, 1)

            def turn_x(n):
                pe.wait_ge(x_ready, n * 16 + 16)
                for k in range(KD):
                    last = pe.transpose(x_ps[k // 4][:, (k % 4) * P:(k % 4 + 1) * P],
                                        x_in[:, k * P:(k + 1) * P], idt[:])
                last.then_inc(x_turned, 1)

            def down(n, p):
                pe.wait_ge(aT_lo_done, n + 1)
                pe.wait_ge(y_done, n)
                for b in range(2):
                    last = times(y_ps[b][:], aT, (wd_hi[p], wd_lo[p]), range(KE), slice(b * NB, (b + 1) * NB))
                last.then_inc(down_done, 1)

            def step(n, p, e=None):
                pe.wait_ge(xT_lo_done, n * 2 + 2)
                pe.wait_ge(silu_done, n)
                for j in range(CHUNKS):
                    if e is not None:
                        pe.wait_ge(g_lo_done, e * CHUNKS + j + 1)
                    last = times(g_ps[:], xT, (wg_hi, wg_lo), range(2 * j, 2 * j + 2), slice(0, DE))
                last.then_inc(gate_done, 1)
                pe.wait_ge(a_done, n + 1)
                turn_a()
                for j in range(CHUNKS):
                    if e is not None:
                        pe.wait_ge(u_lo_done, e * CHUNKS + j + 1)
                    last = times(u_ps[:], xT, (wu_hi, wu_lo), range(2 * j, 2 * j + 2), slice(0, DE))
                last.then_inc(up_done, 1)
                turn_x(n + 1)
                down(n, p)

            pe.wait_ge(idt_in, 16)
            turn_x(0)

            def each(e, p, first_of_all=False):
                first, last = span(pe, e)
                if first_of_all:
                    pe.wait_ge(d_lo_done, CHUNKS)
                    step(first, p, e)
                else:
                    step(first, 1 - p, e)
                    pe.wait_ge(d_lo_done, e * CHUNKS + CHUNKS)
                with pe.If(last > first):
                    with pe.Fori(first + 1, last + 1) as n:
                        step(n, p)

            each(0, 0, first_of_all=True)
            each(1, 1)
            with pe.Fori(1, EXPERTS // 2) as i:
                for p in range(2):
                    each(i * 2 + p, p)
            end = last_of_all(pe) + 1
            pe.wait_ge(a_done, end + 1)
            turn_a()
            down(end, 1)


def combine(nc, x2, ys, norm_final, out, routes):
    with Stage(nc, "cb") as st:
        x_in = [st.sb(f"x_in{p}", [P, D]) for p in range(2)]
        y_in = [[st.sb(f"y_in{p}{k}", [P, D]) for k in range(2)] for p in range(2)]
        done = [st.sb(f"done{p}", [P, D]) for p in range(2)]
        junk = [st.sb(f"junk{p}", [P, D], BF16) for p in range(2)]
        stat = [st.sb(f"stat{p}", [P, 8]) for p in range(2)]
        g_row = st.sb("g_row", [P, D])
        const_in = st.sem("const_in")
        x_ready = [st.sem(f"x_ready{p}") for p in range(2)]
        y_ready = [st.sem(f"y_ready{p}") for p in range(2)]
        summed = st.sem("summed")
        ssq_done, mean_done, root_done, rstd_done = (
            st.sem(n) for n in ("ssq_done", "mean_done", "root_done", "rstd_done"))
        normed = st.sem("normed")
        stored = [st.sem(f"stored{p}") for p in range(2)]
        block = st.block()

        @block.sync
        def _(sp):
            sp.dma_start(g_row[:], norm_final.partition_broadcast(P)).then_inc(const_in, 16)

            def load(t):
                sp.dma_start(x_in[t % 2][:], x2[t * P:(t + 1) * P, :]).then_inc(x_ready[t % 2], 16)

            load(0)
            load(1)
            for t in range(NT):
                sp.wait_ge(normed, t + 1)
                sp.dma_start(out[t * P:(t + 1) * P, :], done[t % 2][:]).then_inc(stored[t % 2], 16)
                if t + 2 < NT:
                    load(t + 2)
            for p in range(2):
                sp.wait_ge(stored[p], 16 * (NT // 2))

        @block.gpsimd
        def _(pool):
            for t in range(NT):
                if t >= 2:
                    pool.wait_ge(summed, 2 * (t - 1))
                for k in range(2):
                    pool.indirect_dma_start(
                        out=y_in[t % 2][k][:], out_offset=None, in_=ys,
                        in_offset=bass.IndirectOffsetOnAxis(ap=routes.slot[k][:, t:t + 1], axis=0)
                    ).then_inc(y_ready[t % 2], 16)

        @block.scalar
        def _(act):
            for t in range(NT):
                p = t % 2
                act.wait_ge(summed, 2 * t + 2)
                act.activation(junk[p][:], x_in[p][:], ACT.Square, accum_out=stat[p][:, 0:1]).then_inc(ssq_done, 1)
                act.wait_ge(mean_done, t + 1)
                act.activation(stat[p][:, 2:3], stat[p][:, 1:2], ACT.Sqrt).then_inc(root_done, 1)

        @block.vector
        def _(dve):
            def add(t):
                p = t % 2
                dve.wait_ge(x_ready[p], 16 * (t // 2 + 1))
                dve.wait_ge(y_ready[p], 32 * (t // 2 + 1))
                for k in range(2):
                    dve.scalar_tensor_tensor(x_in[p][:], y_in[p][k][:], routes.weight[k][:, t:t + 1], x_in[p][:],
                                             ALU.mult, ALU.add).then_inc(summed, 1)
                    dve.wait_ge(summed, 2 * t + k + 1)

            dve.wait_ge(const_in, 16)
            add(0)
            for t in range(NT):
                p = t % 2
                if t + 1 < NT:
                    add(t + 1)
                rms_tail(dve, stat[p], t, ssq_done, mean_done, root_done, rstd_done)
                if t >= 2:
                    dve.wait_ge(stored[p], 16 * (t // 2))
                dve.scalar_tensor_tensor(done[p][:], x_in[p][:], stat[p][:, 6:7], g_row[:],
                                         ALU.mult, ALU.mult).then_inc(normed, 1)


def feature_columns():
    a_q, a_k, a_v, b_q, b_k, b_v = 0, 512, 640, 768, 1280, 1792
    spans = [(b_q, 512), (b_k, 512), (b_v, 512), (a_q, 512), (a_k, 128), (a_v, 128)]
    return np.concatenate([np.arange(s, s + n) for s, n in spans])


def layout(x, norm_mix, w_in, w_branch_gate, b_branch_gate):
    w = np.concatenate([w_in[0][:, feature_columns()], w_branch_gate[0]], axis=1)
    tiles = w.shape[1] // P
    return {
        "x": x.reshape(SEQ, D),
        "norm_mix": norm_mix.reshape(D),
        "w_feat": np.ascontiguousarray(w.reshape(KD, P, tiles, P).transpose(2, 1, 0, 3).reshape(tiles, P, D)),
        "gate_bias": np.ascontiguousarray(b_branch_gate.reshape(GATE_TILES, P).T),
        "ident": np.eye(P, dtype=np.float32),
        **rope_tables(),
    }


def band_b(rel_bias):
    q, k = np.arange(P)[:, None], np.arange(5 * P)[None, :] - 4 * P
    idx = np.clip(q - k, -MAX_REL, MAX_REL) + MAX_REL
    chunks = q // CHUNK - k // CHUNK
    rows = rel_bias[0][:, idx]
    rows = np.where((chunks >= 0) & (chunks <= 8), rows, np.float32(NEG))
    return np.ascontiguousarray(np.concatenate([rows, rows[-1:]]).reshape(-1, 5 * P))


def band_a():
    q, k = np.arange(P)[:, None], np.arange(2 * P)[None, :] - P
    chunks = q // CHUNK - k // CHUNK
    return np.where((chunks >= 0) & (chunks <= 1), np.float32(0), np.float32(NEG))


def rope_tables():
    inv = (10000.0 ** (-np.arange(DH // 2) / (DH // 2))).astype(np.float32)
    angle = inv[np.arange(P) % (DH // 2), None] * np.arange(SEQ, dtype=np.float32)
    sign = np.where(np.arange(P) % DH < DH // 2, -1.0, 1.0)[:, None]
    return {"rope_cos": np.cos(angle.astype(np.float64)).astype(np.float32),
            "rope_sin": (sign * np.sin(angle.astype(np.float64))).astype(np.float32)}


def mix_slabs(w_o_a, w_o_b, w_out):
    return np.ascontiguousarray(np.concatenate([w_o_a[0], w_o_b[0], w_out[0]]).reshape(OUT_SLABS, P, D))


def router_layout(w_router_group, b_router_group, w_router_expert, b_router_expert):
    w = np.concatenate([w_router_group[0], w_router_expert[0]], axis=1)
    return {"w_router": np.ascontiguousarray(w.reshape(KD, P, LOGITS).transpose(1, 0, 2).reshape(P, KD * LOGITS)),
            "b_router": np.concatenate([b_router_group[0], b_router_expert[0]]),
            "strict_upper": np.triu(np.ones((P, P), np.float32), 1),
            "token_ids": np.ascontiguousarray(np.arange(SEQ, dtype=np.float32).reshape(NT, P).T)}


def encoder_block(nc, x, norm_mix, w_feat, gate_bias, rope_cos, rope_sin, ident, band, mask, sinks, w_mix,
                  norm_ffn, w_router, b_router, strict_upper, token_ids, w_exp_gate, w_exp_up, w_exp_down,
                  norm_final, out):
    def scratch(name, shape):
        return nc.dram_tensor(f"scratch_{name}", shape, F32, kind="Internal").ap()

    feat = scratch("feat", (COPY_TILES, P, SEQ))
    rotated = scratch("rotated", (ROPE_TILES * P, SEQ))
    gates = scratch("gates", (GATE_TILES, P, SEQ))
    att = scratch("att", (SEQ + MB, D))
    x2, h2 = scratch("x2", (SEQ, D)), scratch("h2", (SEQ, D))
    table = scratch("table", (MAX_TILES * P, 1))
    ys = scratch("ys", ((MAX_TILES + 1) * P, D))
    sure = (1 + 2 * SEQ // P) * P

    project(nc, x, norm_mix, w_feat, gate_bias, rope_cos, rope_sin, ident, feat, rotated, gates)
    rows = feat.rearrange("a p n -> (a p) n")
    attend_b(nc, rows, band, ident, att, (att[SEQ:, :], ys[sure:, :]))
    attend_a(nc, rows, rotated, mask, sinks, ident, att)
    merge(nc, x, att, gates, w_mix, norm_ffn, ident, x2, h2)
    with Stage(nc, "routes") as st:
        routes = Routes(st)
        route(nc, h2, w_router, b_router, ident, strict_upper, token_ids, table, routes)
        experts(nc, h2, w_exp_gate, w_exp_up, w_exp_down, ident, ys, routes)
        combine(nc, x2, ys, norm_final, out, routes)


def kernel(x, norm_mix, w_in, attn_sinks, rel_bias, w_o_a, w_o_b, w_branch_gate, b_branch_gate, w_out, norm_ffn,
           w_router_group, b_router_group, w_router_expert, b_router_expert, w_exp_gate, w_exp_up, w_exp_down,
           norm_final):
    import concourse.bacc as _bacc
    from concourse.bass_utils import run_bass_kernel_spmd as _run

    (x, norm_mix, w_in, attn_sinks, rel_bias, w_o_a, w_o_b, w_branch_gate, b_branch_gate, w_out, norm_ffn,
     w_router_group, b_router_group, w_router_expert, b_router_expert, w_exp_gate, w_exp_up, w_exp_down,
     norm_final) = (np.asarray(a) for a in (
         x, norm_mix, w_in, attn_sinks, rel_bias, w_o_a, w_o_b, w_branch_gate, b_branch_gate, w_out, norm_ffn,
         w_router_group, b_router_group, w_router_expert, b_router_expert, w_exp_gate, w_exp_up, w_exp_down,
         norm_final))
    laid = {
        **layout(x, norm_mix, w_in, w_branch_gate, b_branch_gate),
        "band": band_b(rel_bias), "mask": band_a(), "sinks": attn_sinks.reshape(HEADS),
        "w_mix": mix_slabs(w_o_a, w_o_b, w_out), "norm_ffn": norm_ffn.reshape(D),
        **router_layout(w_router_group, b_router_group, w_router_expert, b_router_expert),
        "w_exp_gate": w_exp_gate[0], "w_exp_up": w_exp_up[0], "w_exp_down": w_exp_down[0],
        "norm_final": norm_final,
    }
    nc = _bacc.Bacc("TRN2", target_bir_lowering=False, num_devices=1)
    arrays = {f"in_{name}_dram": np.ascontiguousarray(a) for name, a in laid.items()}
    args = {name: nc.dram_tensor(f"in_{name}_dram", a.shape, F32, kind="ExternalInput").ap()
            for name, a in laid.items()}
    out = nc.dram_tensor("out_0_dram", (SEQ, D), F32, kind="ExternalOutput").ap()
    encoder_block(nc, out=out, **args)
    r = _run(nc, [arrays], core_ids=[0])
    return r.results[0]["out_0_dram"].reshape(x.shape)
```

```python
from contextlib import ExitStack

import numpy as np

import concourse.bass as bass
from concourse import mybir

ALU = mybir.AluOpType
ACT = mybir.ActivationFunctionType
AX_X = mybir.AxisListType.X
F32 = mybir.dt.float32
F32R = mybir.dt.float32r
BF16 = mybir.dt.bfloat16
I32 = mybir.dt.int32
U32 = mybir.dt.uint32
ds = bass.ds

P = 128
SEQ = 2048
D = 1024
KD = D // P
NT = SEQ // P
EPS = 1e-6
RSTD_STEPS = 4
NEG = -1e30
NB = 512
COPY_TILES = 18
GATE_TILES = 16
ROPE_FIRST = 12
ROPE_TILES = 5
HALF = SEQ // 2
A_COLS = 512
CHUNK = 64
MAX_REL = 256


class Stage:

    def __init__(self, nc, tag):
        self.nc, self.tag, self.ctx, self.sems = nc, tag, ExitStack(), []

    def __enter__(self):
        return self

    def __exit__(self, *exc):
        self.ctx.close()
        if self.sems:
            self.nc.clear_and_free_semaphores(self.sems)
            self.nc.all_engine_barrier()

    def sb(self, name, shape, dt=F32):
        return self.ctx.enter_context(self.nc.sbuf_tensor(f"{self.tag}_{name}", shape, dt))

    def ps(self, name, shape, dt=F32):
        return self.ctx.enter_context(self.nc.psum_tensor(f"{self.tag}_{name}", shape, dt))

    def sem(self, name):
        self.sems.append(self.nc.alloc_semaphore(f"{self.tag}_{name}"))
        return self.sems[-1]

    def block(self):
        return self.ctx.enter_context(self.nc.Block())


def hold(eng, spare):
    eng.sem_inc(spare, 1)


def mean_square(dve, stat, t, ssq_done, mean_done):
    dve.wait_ge(ssq_done, t + 1)
    dve.tensor_scalar(stat[:, 1:2], stat[:, 0:1], 1.0 / D, EPS, ALU.mult, ALU.add).then_inc(mean_done, 1)


def root(act, stat, t, mean_done, root_done):
    act.wait_ge(mean_done, t + 1)
    act.activation(stat[:, 2:3], stat[:, 1:2], ACT.Sqrt).then_inc(root_done, 1)


def inverse_rms(dve, stat, t, root_done, rstd_done):
    dve.wait_ge(root_done, t + 1)
    dve.reciprocal(stat[:, 5:6], stat[:, 2:3]).then_inc(rstd_done, 1)
    dve.wait_ge(rstd_done, t * RSTD_STEPS + 1)
    dve.scalar_tensor_tensor(stat[:, 3:4], stat[:, 5:6], stat[:, 5:6], stat[:, 1:2],
                             ALU.mult, ALU.mult).then_inc(rstd_done, 1)
    dve.wait_ge(rstd_done, t * RSTD_STEPS + 2)
    dve.tensor_scalar(stat[:, 6:7], stat[:, 3:4], -0.5, 1.5, ALU.mult, ALU.add).then_inc(rstd_done, 1)
    dve.wait_ge(rstd_done, t * RSTD_STEPS + 3)
    dve.tensor_tensor(stat[:, 4:5], stat[:, 5:6], stat[:, 6:7], ALU.mult).then_inc(rstd_done, 1)
    dve.wait_ge(rstd_done, t * RSTD_STEPS + 4)


def project(nc, x, norm_mix, w_feat, gate_bias, rope_cos, rope_sin, ident, feat, rotated, gates):
    with Stage(nc, "pj") as st:
        hT_hi = st.sb("hT_hi", [P, KD, SEQ], F32R)
        hT_lo = st.sb("hT_lo", [P, KD, SEQ], F32R)
        x_in = [st.sb(f"x_in{p}", [P, D]) for p in range(4)]
        w_raw = [st.sb(f"w_raw{p}", [P, D]) for p in range(2)]
        w_hi = [st.sb(f"w_hi{p}", [P, D], F32R) for p in range(2)]
        w_lo = [st.sb(f"w_lo{p}", [P, D], F32R) for p in range(2)]
        f_out = [st.sb(f"f_out{p}", [P, HALF]) for p in range(2)]
        g_row = st.sb("g_row", [P, D])
        idt = st.sb("idt", [P, P])
        ro_raw, ro_swap, ro_cos, ro_sin, ro_out = (
            st.sb(n, [P, NB]) for n in ("ro_raw", "ro_swap", "ro_cos", "ro_sin", "ro_out"))
        gbias = st.sb("gbias", [P, GATE_TILES])
        stat = [st.sb(f"stat{p}", [P, 8]) for p in range(4)]
        eight = [st.ps(f"bank{b}", [P, NB]) for b in range(8)]

        junk = [st.sb(f"junk{p}", [P, D], BF16) for p in range(2)]
        held = st.sem("held")
        const_in = st.sem("const_in")
        x_ready = [st.sem(f"x_ready{p}") for p in range(4)]
        ssq_done = st.sem("ssq_done")
        mean_done = st.sem("mean_done")
        root_done = st.sem("root_done")
        rstd_done = st.sem("rstd_done")
        xg_done = st.sem("xg_done")
        h_done = st.sem("h_done")
        tr_done = st.sem("tr_done")
        hi_done = st.sem("hi_done")
        tr_read = st.sem("tr_read")
        w_ready = [st.sem(f"w_ready{p}") for p in range(2)]
        whi_done = st.sem("whi_done")
        wlo_done = st.sem("wlo_done")
        mm_done = st.sem("mm_done")
        evacuated = st.sem("evacuated")
        stored = [st.sem(f"stored{p}") for p in range(2)]
        ro_in, ro_done, ro_stored = st.sem("ro_in"), st.sem("ro_done"), st.sem("ro_stored")
        block = st.block()
        TILES = COPY_TILES + GATE_TILES

        @block.sync
        def _(sp):
            for half in range(2):
                sp.sem_inc(stored[half], 16)
            sp.dma_start(g_row[:], norm_mix.partition_broadcast(P)).then_inc(const_in, 16)
            sp.dma_start(idt[:], ident).then_inc(const_in, 16)
            sp.dma_start(gbias[:], gate_bias).then_inc(const_in, 16)
            for p in range(4):
                sp.dma_start(x_in[p][:], x[p * P:(p + 1) * P, :]).then_inc(x_ready[p], 16)
            for p in range(2):
                sp.dma_start(w_raw[p][:], w_feat[p]).then_inc(w_ready[p], 16)
            with sp.Fori(1, NT // 4) as i:
                for p in range(4):
                    sp.wait_ge(tr_done, i * 4 + p - 3)
                    sp.dma_start(x_in[p][:], x[ds((i * 4 + p) * P, P), :]).then_inc(x_ready[p], 16)

            def store(dst, i, first, more=True):
                for p in range(2):
                    if more:
                        sp.wait_ge(wlo_done, i * 2 + p + first + 1)
                        sp.dma_start(w_raw[p][:], w_feat[ds(i * 2 + p + first + 2, 1), :, :].rearrange(
                            "a p n -> (a p) n")).then_inc(w_ready[p], 16)
                    for half in range(2):
                        sp.wait_ge(evacuated, (i * 2 + p + first) * 4 + 8 + 2 * half + 2)
                        sp.dma_start(dst[ds(i * 2 + p, 1), :, half * HALF:(half + 1) * HALF]
                                     .rearrange("a p n -> (a p) n"), f_out[half][:]).then_inc(stored[half], 16)

            with sp.Fori(0, COPY_TILES // 2) as i:
                store(feat, i, 0)
            with sp.Fori(0, GATE_TILES // 2 - 1) as i:
                store(gates, i, COPY_TILES)
            with sp.Fori(GATE_TILES // 2 - 1, GATE_TILES // 2) as i:
                store(gates, i, COPY_TILES, more=False)
            for half in range(2):
                sp.wait_ge(stored[half], 16 * TILES + 16)

        @block.gpsimd
        def _(pool):
            pool.wait_ge(const_in, 48)
            with pool.Fori(0, NT // 4) as i:
                for p in range(4):
                    pool.wait_ge(ssq_done, i * 4 + p + 1)
                    pool.tensor_tensor(x_in[p][:], x_in[p][:], g_row[:], ALU.mult).then_inc(xg_done, 1)
            for r in range(ROPE_TILES):
                for half in range(2):
                    pool.wait_ge(stored[half], 16 * (ROPE_FIRST + r + 2))
                with pool.Fori(0, SEQ // NB) as c:
                    cols = ds(c * NB, NB)
                    pool.dma_start(ro_raw[:], feat[ROPE_FIRST + r, :, cols]).then_inc(ro_in, 16)
                    for q in range(4):
                        src = (q ^ 1) * 32
                        pool.dma_start(ro_swap[q * 32:q * 32 + 32, :],
                                       feat[ROPE_FIRST + r, src:src + 32, cols]).then_inc(ro_in, 16)
                    pool.dma_start(ro_cos[:], rope_cos[:, cols]).then_inc(ro_in, 16)
                    pool.dma_start(ro_sin[:], rope_sin[:, cols]).then_inc(ro_in, 16)
                    pool.wait_ge(ro_in, (c + r * (SEQ // NB)) * 112 + 112)
                    pool.tensor_tensor(ro_out[:], ro_raw[:], ro_cos[:], ALU.mult).then_inc(ro_done, 1)
                    pool.tensor_tensor(ro_swap[:], ro_swap[:], ro_sin[:], ALU.mult).then_inc(ro_done, 1)
                    pool.wait_ge(ro_done, (c + r * (SEQ // NB)) * 3 + 2)
                    pool.tensor_tensor(ro_out[:], ro_out[:], ro_swap[:], ALU.add).then_inc(ro_done, 1)
                    pool.wait_ge(ro_done, (c + r * (SEQ // NB)) * 3 + 3)
                    hold(pool, held)
                    pool.dma_start(rotated[r * P:(r + 1) * P, cols], ro_out[:]).then_inc(ro_stored, 16)
                    pool.wait_ge(ro_stored, (c + r * (SEQ // NB)) * 16 + 16)

        @block.scalar
        def _(act):
            def scale(t, p):
                act.wait_ge(xg_done, t + 1)
                hold(act, held)
                act.wait_ge(rstd_done, t * RSTD_STEPS + RSTD_STEPS)
                hold(act, held)
                act.activation(x_in[p][:], x_in[p][:], ACT.Copy, scale=stat[p][:, 4:5]).then_inc(h_done, 1)

            def over_tiles(i, more=True):
                for p in range(4):
                    if more or p < 3:
                        scale(i * 4 + p + 1, (p + 1) % 4)
                    if more or p < 2:
                        root(act, stat[(p + 2) % 4], i * 4 + p + 2, mean_done, root_done)
                    act.wait_ge(tr_done, i * 4 + p + 1)
                    hold(act, held)
                    for b in range(2):
                        act.activation(hT_hi[:, 4 * b:4 * b + 4, ds((i * 4 + p) * P, P)],
                                       eight[2 * p + b][:].rearrange("p (k t) -> p k t", k=4),
                                       ACT.Copy).then_inc(hi_done, 1)

            root(act, stat[0], 0, mean_done, root_done)
            root(act, stat[1], 1, mean_done, root_done)
            scale(0, 0)
            with act.Fori(0, NT // 4 - 1) as i:
                over_tiles(i)
            with act.Fori(NT // 4 - 1, NT // 4) as i:
                over_tiles(i, more=False)

            def split_weights(i, p):
                act.wait_ge(w_ready[p], i * 16 + 16)
                act.wait_ge(mm_done, i * 2 + p + 1)
                act.activation(w_hi[p][:], w_raw[p][:], ACT.Copy).then_inc(whi_done, 1)

            def evacuate(i, p, first, func):
                act.wait_ge(mm_done, i * 2 + p + first + 3)
                for half in range(2):
                    act.wait_ge(stored[half], (i * 2 + p + first) * 16 + 16)
                    if func == ACT.Sigmoid:
                        hold(act, held)
                    for b in range(2):
                        bias = gbias[:, ds(i * 2 + p, 1)] if func == ACT.Sigmoid else 0.0
                        act.activation(f_out[half][:, b * NB:(b + 1) * NB], eight[4 * p + 2 * half + b][:],
                                       func, bias=bias).then_inc(evacuated, 1)

            split_weights(0, 0)
            split_weights(0, 1)
            with act.Fori(0, COPY_TILES // 2) as i:
                for p in range(2):
                    evacuate(i, p, 0, ACT.Copy)
                    split_weights(i + 1, p)
            act.wait_ge(const_in, 48)
            with act.Fori(0, GATE_TILES // 2 - 1) as i:
                for p in range(2):
                    evacuate(i, p, COPY_TILES, ACT.Sigmoid)
                    split_weights(i + (COPY_TILES // 2 + 1), p)
            with act.Fori(GATE_TILES // 2 - 1, GATE_TILES // 2) as i:
                for p in range(2):
                    evacuate(i, p, COPY_TILES, ACT.Sigmoid)

        @block.vector
        def _(dve):
            def square(i, p):
                dve.wait_ge(x_ready[p], i * 16 + 16)
                hold(dve, held)
                dve.tensor_tensor_reduce(junk[p % 2][:], x_in[p][:], x_in[p][:], 1.0, 0.0, ALU.mult, ALU.add,
                                         stat[p][:, 0:1]).then_inc(ssq_done, 1)
                mean_square(dve, stat[p], i * 4 + p, ssq_done, mean_done)

            def over_tiles(i, more=True):
                for p in range(4):
                    if more or p < 3:
                        inverse_rms(dve, stat[(p + 1) % 4], i * 4 + p + 1, root_done, rstd_done)
                    if more or p < 2:
                        square(i + p // 2, (p + 2) % 4)
                    for b in range(2):
                        dve.wait_ge(hi_done, i * 8 + 2 * p + b + 1)
                        where = (slice(None), slice(4 * b, 4 * b + 4), ds((i * 4 + p) * P, P))
                        dve.tensor_tensor(hT_lo[where], eight[2 * p + b][:].rearrange("p (k t) -> p k t", k=4),
                                          hT_hi[where], ALU.subtract).then_inc(tr_read, 1)

            square(0, 0)
            square(0, 1)
            inverse_rms(dve, stat[0], 0, root_done, rstd_done)
            with dve.Fori(0, NT // 4 - 1) as i:
                over_tiles(i)
            with dve.Fori(NT // 4 - 1, NT // 4) as i:
                over_tiles(i, more=False)
            with dve.Fori(0, TILES // 2) as i:
                for p in range(2):
                    dve.wait_ge(whi_done, i * 2 + p + 1)
                    dve.tensor_tensor(w_lo[p][:], w_raw[p][:], w_hi[p][:], ALU.subtract).then_inc(wlo_done, 1)

        @block.tensor
        def _(pe):
            pe.sem_inc(tr_read, 8)
            pe.sem_inc(mm_done, 2)
            pe.sem_inc(evacuated, 8)
            pe.wait_ge(const_in, 48)
            with pe.Fori(0, NT // 4) as i:
                for p in range(4):
                    pe.wait_ge(h_done, i * 4 + p + 1)
                    pe.wait_ge(tr_read, i * 8 + 2 * p + 2)
                    for k in range(KD):
                        last = pe.transpose(eight[2 * p + k // 4][:, (k % 4) * P:(k % 4 + 1) * P],
                                            x_in[p][:, k * P:(k + 1) * P], idt[:])
                    last.then_inc(tr_done, 1)
            pe.wait_ge(tr_read, 2 * NT + 8)
            with pe.Fori(0, TILES // 2) as i:
                for p in range(2):
                    pe.wait_ge(wlo_done, i * 2 + p + 1)
                    pe.wait_ge(evacuated, (i * 2 + p) * 4 + 4)
                    for k in range(KD):
                        for n, (w, h) in enumerate(((w_hi, hT_hi), (w_hi, hT_lo), (w_lo, hT_hi))):
                            for b in range(4):
                                last = pe.matmul(eight[4 * p + b][:], w[p][:, k * P:(k + 1) * P],
                                                 h[:, k, b * NB:(b + 1) * NB],
                                                 start=(k == 0 and n == 0), stop=(k == KD - 1 and n == 2))
                    last.then_inc(mm_done, 1)


HEADS = 8
DH = 64
NPAIR = HEADS // 2
UNITS = 2 * NT
PARTS = 4
SPLIT_STEP = 7
V_STEPS = (12, 14)
V_PARTS = 2


def attend(nc, tag, q_rows, k_rows, v_rows, head_of, shared_kv, key_tiles, bias, sinks, ident, att, att_col, blank=None):
    KW = key_tiles * P
    with Stage(nc, tag) as st:
        k_raw = st.sb("k_raw", [P, SEQ])
        q_raw = st.sb("q_raw", [P, SEQ])
        v_raw = st.sb("v_raw", [DH, SEQ])
        k_st = [st.sb(f"k_st{p}", [P, SEQ], F32R) for p in range(2)]
        q_hi = [st.sb(f"q_hi{p}", [P, SEQ], F32R) for p in range(2)]
        q_lo = [st.sb(f"q_lo{p}", [P, SEQ], F32R) for p in range(2)]
        v_st = [st.sb(f"v_st{p}", [P, NT, 2, DH], F32R) for p in range(2)]
        bias_sb = [st.sb(f"bias{p}", [P, KW]) for p in range(2)]
        prob = [st.sb(f"prob{p}", [P, KW]) for p in range(4)]
        pt_hi = [st.sb(f"pt_hi{p}", [P, KW], F32R) for p in range(2)]
        pt_lo = [st.sb(f"pt_lo{p}", [P, KW], F32R) for p in range(2)]
        o_head = [st.sb(f"o_head{p}", [P, NT, DH]) for p in range(2)]
        idt = st.sb("idt", [P, P])
        sink = st.sb("sink", [P, HEADS])
        top = st.sb("top", [P, UNITS])
        neg = st.sb("neg", [P, UNITS])
        total = st.sb("total", [P, UNITS])
        sink_p = st.sb("sink_p", [P, UNITS])
        full = st.sb("full", [P, UNITS])
        inv = st.sb("inv", [P, UNITS])
        s_ps = st.ps("s_ps", [P, 2 * NB])
        pt_ps = [st.ps(f"pt_ps{p}", [P, 2 * NB]) for p in range(2)]
        o_ps = [st.ps(f"o_ps{p}", [P, NB]) for p in range(2)]
        v_ps = pt_ps[1][:].rearrange("p (n d) -> p n d", d=DH)

        held = st.sem("held")
        const_in = st.sem("const_in")
        q_in = st.sem("q_in")
        kv_in = st.sem("kv_in")
        q_hi_done = st.sem("q_hi_done")
        q_lo_done = st.sem("q_lo_done")
        k_hi_done = st.sem("k_hi_done")
        k_lo_done = st.sem("k_lo_done")
        v_tr = st.sem("v_tr")
        v_hi_done = st.sem("v_hi_done")
        v_lo_done = st.sem("v_lo_done")
        scored = st.sem("scored")
        maxed = st.sem("maxed")
        neg_done = st.sem("neg_done")
        exped = st.sem("exped")
        sink_done = st.sem("sink_done")
        transposed = st.sem("transposed")
        pt_hi_done = st.sem("pt_hi_done")
        pt_lo_done = st.sem("pt_lo_done")
        valued = st.sem("valued")
        full_done = st.sem("full_done")
        inv_done = st.sem("inv_done")
        o_done = st.sem("o_done")
        o_copied = st.sem("o_copied")
        head_done = st.sem("head_done")
        att_out = [st.sem(f"att_out{p}") for p in range(2)]
        block = st.block()
        with_sink = sinks is not None
        kv_heads = 2 if shared_kv else HEADS
        CONSTS = 16 * (1 + with_sink + 2 * shared_kv)

        def ahead(step, j, u, n, more):
            if u + n < UNITS:
                step(j, u + n)
            elif more:
                step(j + 1, u + n - UNITS)

        def over_pairs(eng, each):
            with eng.Fori(0, NPAIR - 1) as j:
                each(j, True)
            with eng.Fori(NPAIR - 1, NPAIR) as j:
                each(j, False)

        def v_tiles(c):
            return slice(c * (NT // V_PARTS), (c + 1) * (NT // V_PARTS))

        def part(c):
            return slice(c * (SEQ // PARTS), (c + 1) * (SEQ // PARTS))

        def tiles_of(n):
            m = min(n + 1, key_tiles)
            return n + 1 - m, m

        @block.sync
        def _(sp):
            def load_q(pair, hh):
                for half in range(2):
                    sp.dma_start(q_raw[half * DH:(half + 1) * DH, :], q_rows(pair, hh)).then_inc(q_in, 16)
                if not shared_kv:
                    sp.dma_start(bias_sb[hh][:], bias(pair, hh)).then_inc(q_in, 16)

            def load_kv(pair, hh):
                for half in range(2):
                    sp.dma_start(k_raw[half * DH:(half + 1) * DH, :], k_rows(pair, hh)).then_inc(kv_in, 16)
                sp.dma_start(v_raw[:], v_rows(pair, hh)).then_inc(kv_in, 16)

            for hh in range(2):
                sp.sem_inc(att_out[hh], 16)
            sp.dma_start(idt[:], ident).then_inc(const_in, 16)
            if with_sink:
                sp.dma_start(sink[:], sinks.partition_broadcast(P)).then_inc(const_in, 16)
            if shared_kv:
                for p in range(2):
                    sp.dma_start(bias_sb[p][:], bias(0, p)).then_inc(const_in, 16)
            load_kv(0, 0)
            load_q(0, 0)
            if shared_kv:
                sp.wait_ge(k_lo_done, PARTS)
                sp.wait_ge(v_tr, V_PARTS)
                load_kv(0, 1)
            with sp.Fori(0, NPAIR) as j:
                for hh in range(2):
                    sp.wait_ge(q_lo_done, (j * 2 + hh + 1) * PARTS)
                    hold(sp, held)
                    if not shared_kv:
                        sp.wait_ge(k_lo_done, (j * 2 + hh + 1) * PARTS)
                        hold(sp, held)
                        sp.wait_ge(v_tr, (j * 2 + hh + 1) * V_PARTS)
                        hold(sp, held)
                        sp.wait_ge(maxed, (j * 2 + hh) * NT + 1)
                    nj, nh = (j, 1) if hh == 0 else (j + 1, 0)
                    hold(sp, held)
                    load_q(nj, nh)
                    if not shared_kv:
                        load_kv(nj, nh)
                    sp.wait_ge(head_done, j * 2 + hh + 1)
                    hold(sp, held)
                    dst = att[:SEQ, ds(head_of(j, hh) * DH + att_col, DH)].rearrange("(n p) d -> p n d", p=P)
                    sp.dma_start(dst, o_head[hh][:]).then_inc(att_out[hh], 16)
            for hh in range(2):
                sp.wait_ge(att_out[hh], 16 * NPAIR + 16)
            sp.wait_ge(q_in, (HEADS + 1) * 16 * (2 if shared_kv else 3))
            sp.wait_ge(kv_in, (2 if shared_kv else HEADS + 1) * 48)

        if blank is not None:
            zeros = st.sb("zeros", [P, D])
            zeros_set, blanked = st.sem("zeros_set"), st.sem("blanked")

        @block.gpsimd
        def _(pool):
            def split_k(h, hh):
                for c in range(PARTS):
                    pool.wait_ge(k_hi_done, h * PARTS + c + 1)
                    pool.tensor_tensor(k_st[hh][DH:P, part(c)], k_raw[DH:P, part(c)], k_st[hh][DH:P, part(c)],
                                       ALU.subtract).then_inc(k_lo_done, 1)

            split_k(0, 0)
            if shared_kv:
                split_k(1, 1)
            if blank is not None:
                pool.wait_ge(k_lo_done, PARTS * (2 if shared_kv else 1))
                pool.memset(zeros[:], 0.0).then_inc(zeros_set, 1)
                pool.wait_ge(zeros_set, 1)
                tiles = sum(rows.shape[0] for rows in blank) // P
                for rows in blank:
                    with pool.Fori(0, rows.shape[0] // P) as t:
                        pool.dma_start(rows[ds(t * P, P), :], zeros[:]).then_inc(blanked, 16)
                pool.wait_ge(blanked, tiles * 16)
            if not shared_kv:
                with pool.Fori(0, NPAIR) as j:
                    for hh in range(2):
                        split_k(j * 2 + hh + 1, 1 - hh)

        @block.scalar
        def _(act):
            def split_q(h, hh, c):
                act.wait_ge(q_in, (h + 1) * (32 if shared_kv else 48))
                act.activation(q_hi[hh][:, part(c)], q_raw[:, part(c)], ACT.Copy, scale=0.125).then_inc(q_hi_done, 1)

            def split_k(h, hh, c):
                act.wait_ge(kv_in, (h + 1) * 48)
                act.activation(k_st[hh][:, part(c)], k_raw[:, part(c)], ACT.Copy).then_inc(k_hi_done, 1)

            def split_v(h, hh, c):
                act.wait_ge(v_tr, h * V_PARTS + c + 1)
                act.activation(v_st[hh][:, v_tiles(c), 0, :], v_ps[:, v_tiles(c), :], ACT.Copy).then_inc(v_hi_done, 1)

            def exp(j, u):
                hh = u // NT
                w = tiles_of(u % NT)[1] * P
                act.wait_ge(neg_done, j * UNITS + u + 1)
                act.activation(prob[u % 4][:, :w], prob[u % 4][:, :w], ACT.Exp, bias=neg[:, u:u + 1],
                               accum_out=total[:, u:u + 1]).then_inc(exped, 1)
                if with_sink and u % NT == NT - 1:
                    act.wait_ge(const_in, CONSTS)
                    hold(act, held)
                    head = slice(hh * NT, (hh + 1) * NT)
                    act.activation(sink_p[:, head], neg[:, head], ACT.Exp,
                                   bias=sink[:, ds(head_of(j, hh), 1)]).then_inc(sink_done, 1)

            def pt(j, u):
                w = tiles_of(u % NT)[1] * P
                act.wait_ge(transposed, j * UNITS + u + 5)
                act.wait_ge(valued, j * UNITS + u + 1)
                act.activation(pt_hi[u % 2][:, :w], pt_ps[u % 2][:, :w], ACT.Copy).then_inc(pt_hi_done, 1)

            for c in range(PARTS):
                split_k(0, 0, c)
            for c in range(PARTS):
                split_q(0, 0, c)
            for c in range(V_PARTS):
                split_v(0, 0, c)
            if shared_kv:
                for c in range(PARTS):
                    split_k(1, 1, c)
                for c in range(V_PARTS):
                    split_v(1, 1, c)
            def each(j, more):
                for u in range(UNITS):
                    ahead(exp, j, u, 1, more)
                    pt(j, u)
                    if SPLIT_STEP <= u % NT < SPLIT_STEP + PARTS:
                        h, hh = j * 2 + u // NT + 1, 1 - u // NT
                        if u % NT == SPLIT_STEP:
                            act.wait_ge(valued, (h - 1) * NT + 2)
                        split_q(h, hh, u % NT - SPLIT_STEP)
                        if not shared_kv:
                            split_k(h, hh, u % NT - SPLIT_STEP)
                    if u % NT in V_STEPS and not shared_kv:
                        split_v(j * 2 + u // NT + 1, 1 - u // NT, V_STEPS.index(u % NT))

            exp(0, 0)
            over_pairs(act, each)

        @block.vector
        def _(dve):
            def split_q(h, hh, c):
                dve.wait_ge(q_hi_done, h * PARTS + c + 1)
                dve.scalar_tensor_tensor(q_lo[hh][:, part(c)], q_raw[:, part(c)], 0.125, q_hi[hh][:, part(c)],
                                         ALU.mult, ALU.subtract).then_inc(q_lo_done, 1)

            def split_v(h, hh, c):
                dve.wait_ge(v_hi_done, h * V_PARTS + c + 1)
                dve.tensor_tensor(v_st[hh][:, v_tiles(c), 1, :], v_ps[:, v_tiles(c), :],
                                  v_st[hh][:, v_tiles(c), 0, :], ALU.subtract).then_inc(v_lo_done, 1)

            def biased(j, u):
                hh = u // NT
                m = tiles_of(u % NT)[1]
                w, skip = m * P, (key_tiles - m) * P
                if u % NT == 0 and not shared_kv:
                    dve.wait_ge(q_in, (j * 2 + hh + 1) * 48)
                dve.wait_ge(scored, j * UNITS + u + 1)
                dve.wait_ge(transposed, j * UNITS + u + 1)
                hold(dve, held)
                dve.tensor_tensor_reduce(prob[u % 4][:, :w], s_ps[:, :w], bias_sb[hh][:, skip:], 1.0, -3e38,
                                         ALU.add, ALU.max, top[:, u:u + 1]).then_inc(maxed, 1)
                dve.wait_ge(maxed, j * UNITS + u + 2)
                if with_sink:
                    dve.wait_ge(const_in, CONSTS)
                floor = sink[:, ds(head_of(j, hh), 1)] if with_sink else -3e38
                dve.tensor_scalar(neg[:, u:u + 1], top[:, u:u + 1], floor, -1.0,
                                  ALU.max, ALU.mult).then_inc(neg_done, 1)

            def pt(j, u):
                w = tiles_of(u % NT)[1] * P
                dve.wait_ge(pt_hi_done, j * UNITS + u + 1)
                dve.tensor_tensor(pt_lo[u % 2][:, :w], pt_ps[u % 2][:, :w], pt_hi[u % 2][:, :w],
                                  ALU.subtract).then_inc(pt_lo_done, 1)

            def collect(j, u):
                hh, n = u // NT, u % NT
                dve.wait_ge(valued, j * UNITS + u + 3)
                if n == 0:
                    dve.wait_ge(att_out[hh], j * 16 + 16)
                dve.tensor_copy(o_head[hh][:, n, :], o_ps[u % 2][:, :DH]).then_inc(o_copied, 1)
                dve.wait_ge(o_copied, j * UNITS + u + 1)
                dve.tensor_tensor(o_head[hh][:, n, :], o_ps[u % 2][:, DH:2 * DH], o_head[hh][:, n, :],
                                  ALU.add).then_inc(o_done, 1)
                if n == NT - 1:
                    normalise(j, hh)

            def normalise(j, hh):
                head = slice(hh * NT, (hh + 1) * NT)
                dve.wait_ge(exped, j * UNITS + (hh + 1) * NT)
                if with_sink:
                    dve.wait_ge(sink_done, j * 2 + hh + 1)
                    dve.tensor_tensor(full[:, head], total[:, head], sink_p[:, head], ALU.add).then_inc(full_done, 1)
                    dve.wait_ge(full_done, j * 2 + hh + 1)
                dve.reciprocal(inv[:, head], (full if with_sink else total)[:, head]).then_inc(inv_done, 1)
                dve.wait_ge(inv_done, j * 2 + hh + 1)
                dve.wait_ge(o_done, j * UNITS + (hh + 1) * NT + 2)
                dve.tensor_tensor(o_head[hh][:], o_head[hh][:],
                                  inv[:, head].unsqueeze(2).broadcast_to([P, NT, DH]), ALU.mult).then_inc(head_done, 1)

            for c in range(PARTS):
                split_q(0, 0, c)
            for c in range(V_PARTS):
                split_v(0, 0, c)
            if shared_kv:
                for c in range(V_PARTS):
                    split_v(1, 1, c)
            def each(j, more):
                for u in range(UNITS):
                    ahead(biased, j, u, 2, more)
                    pt(j, u)
                    if u > 0:
                        collect(j, u - 1)
                    if SPLIT_STEP <= u % NT < SPLIT_STEP + PARTS:
                        split_q(j * 2 + u // NT + 1, 1 - u // NT, u % NT - SPLIT_STEP)
                    if u % NT in V_STEPS and not shared_kv:
                        split_v(j * 2 + u // NT + 1, 1 - u // NT, V_STEPS.index(u % NT))
                collect(j, UNITS - 1)

            biased(0, 0)
            biased(0, 1)
            over_pairs(dve, each)

        @block.tensor
        def _(pe):
            pe.sem_inc(maxed, 1)
            pe.sem_inc(transposed, 4)
            pe.sem_inc(pt_lo_done, 2)
            pe.sem_inc(valued, 2)
            pe.sem_inc(o_done, 2)

            def turn_v(h, c):
                pe.wait_ge(kv_in, (h + 1) * 48)
                hold(pe, held)
                for n in range(NT)[v_tiles(c)]:
                    last = pe.transpose(v_ps[:, n, :], v_raw[:, n * P:(n + 1) * P], idt[:DH, :DH])
                last.then_inc(v_tr, 1)

            def scores(j, u):
                hh, n = u // NT, u % NT
                first, m = tiles_of(n)
                if n == 0:
                    pe.wait_ge(q_lo_done, (j * 2 + hh + 1) * PARTS)
                    if shared_kv:
                        pe.wait_ge(k_lo_done, 2 * PARTS)
                    else:
                        pe.wait_ge(k_lo_done, (j * 2 + hh + 1) * PARTS)
                pe.wait_ge(maxed, j * UNITS + u + 1)
                for c in range(0, m * P, NB):
                    w = min(NB, m * P - c)
                    keys = k_st[hh][:, first * P + c:first * P + c + w]
                    pe.matmul(s_ps[:, c:c + w], q_hi[hh][:, n * P:(n + 1) * P], keys, start=True, stop=False)
                    last = pe.matmul(s_ps[:, c:c + w], q_lo[hh][:, n * P:(n + 1) * P], keys,
                                     start=False, stop=True)
                last.then_inc(scored, 1)

            def turn_p(j, u):
                m = tiles_of(u % NT)[1]
                pe.wait_ge(exped, j * UNITS + u + 1)
                pe.wait_ge(pt_lo_done, j * UNITS + u + 1)
                if shared_kv:
                    pe.wait_ge(v_lo_done, 2 * V_PARTS)
                elif (u - 1) % NT in V_STEPS or u == 0:
                    before = sum(step % NT in V_STEPS for step in range(u))
                    pe.wait_ge(v_lo_done, (j * 2 + 1) * V_PARTS + before)
                for i in range(m):
                    last = pe.transpose(pt_ps[u % 2][:, i * P:(i + 1) * P], prob[u % 4][:, i * P:(i + 1) * P], idt[:])
                last.then_inc(transposed, 1)

            def values(j, u):
                hh = u // NT
                first, m = tiles_of(u % NT)
                if u % NT == 0:
                    if shared_kv:
                        pe.wait_ge(v_lo_done, 2 * V_PARTS)
                    else:
                        pe.wait_ge(v_lo_done, (j * 2 + hh + 1) * V_PARTS)
                pe.wait_ge(pt_lo_done, j * UNITS + u + 3)
                pe.wait_ge(o_done, j * UNITS + u + 1)
                o = o_ps[u % 2]
                for i in range(m):
                    cols = slice(i * P, (i + 1) * P)
                    pe.matmul(o[:, :P], pt_hi[u % 2][:, cols], v_st[hh][:, first + i, :, :].rearrange("p a d -> p (a d)"),
                              start=(i == 0), stop=False)
                    last = pe.matmul(o[:, :P], pt_lo[u % 2][:, cols], v_st[hh][:, first + i, :, :].rearrange("p a d -> p (a d)"),
                                     start=False, stop=(i == m - 1))
                last.then_inc(valued, 1)

            pe.wait_ge(const_in, CONSTS)
            for c in range(V_PARTS):
                turn_v(0, c)
            if shared_kv:
                pe.wait_ge(v_lo_done, V_PARTS)
                for c in range(V_PARTS):
                    turn_v(1, c)
            def each(j, more):
                for u in range(UNITS):
                    turn_p(j, u)
                    if u > 0:
                        values(j, u - 1)
                    ahead(scores, j, u, 3, more)
                    if u % NT in V_STEPS and not shared_kv:
                        pe.wait_ge(pt_lo_done, j * UNITS + u + 2)
                        turn_v(j * 2 + u // NT + 1, V_STEPS.index(u % NT))
                values(j, UNITS - 1)

            for u in range(3):
                scores(0, u)
            over_pairs(pe, each)


def attend_b(nc, feat, band, ident, att):
    rows = lambda tile: lambda j, hh: feat[ds(j * P + (tile * P + hh * DH), DH), :]
    attend(nc, "b", rows(0), rows(4), rows(8), lambda j, hh: j * 2 + hh, False, 5,
           lambda j, hh: band[ds((j * 2 + hh) * P, P), :], None, ident, att, A_COLS)


def attend_a(nc, feat, rotated, mask, sinks, ident, att, blank=None):
    attend(nc, "a", lambda j, hh: rotated[ds(j * DH + 4 * DH * hh, DH), :],
           lambda j, hh: rotated[(4 * P + hh * DH):(4 * P + hh * DH) + DH, :],
           lambda j, hh: feat[(17 * P + hh * DH):(17 * P + hh * DH) + DH, :],
           lambda j, hh: j + 4 * hh, True, 2, lambda j, hh: mask, sinks, ident, att, 0, blank)


MB = 256
OUT_SLABS = 16


def merge(nc, x, att, gates, w_mix, norm_ffn, ident, x2, h2):
    with Stage(nc, "mg") as st:
        w_hi = st.sb("w_hi", [P, OUT_SLABS, D], F32R)
        w_lo = st.sb("w_lo", [P, OUT_SLABS, D], F32R)
        w_raw = [st.sb(f"w_raw{p}", [P, D]) for p in range(2)]
        att_in = [st.sb(f"att_in{p}", [P, D]) for p in range(2)]
        aT_hi = st.sb("aT_hi", [P, KD, MB], F32R)
        aT_lo = st.sb("aT_lo", [P, KD, MB], F32R)
        mix_hi = st.sb("mix_hi", [P, KD, MB], F32R)
        mix_lo = st.sb("mix_lo", [P, KD, MB], F32R)
        g_in = [st.sb(f"g_in{p}", [P, 2 * MB]) for p in range(2)]
        gated = [st.sb(f"gated{p}", [P, 2 * MB]) for p in range(2)]
        mixed = [st.sb(f"mixed{p}", [P, MB]) for p in range(2)]
        x_t = [st.sb(f"x_t{p}", [P, D]) for p in range(2)]
        h_t = st.sb("h_t", [P, D])
        junk = st.sb("junk", [P, D], BF16)
        g_row = st.sb("g_row", [P, D])
        idt = st.sb("idt", [P, P])
        stat = [st.sb(f"stat{p}", [P, 8]) for p in range(2)]
        t_ps = [st.ps(f"t_ps{b}", [P, NB]) for b in range(2)]
        y_ps = [st.ps(f"y_ps{b}", [P, 2, MB]) for b in range(2)]
        o_ps = [[st.ps(f"o_ps{t}{b}", [P, NB]) for b in range(2)] for t in range(2)]

        held = st.sem("held")
        const_in = st.sem("const_in")
        w_in = [st.sem(f"w_in{p}") for p in range(2)]
        w_hi_done = st.sem("w_hi_done")
        w_lo_done = st.sem("w_lo_done")
        att_ready = [st.sem(f"att_ready{p}") for p in range(2)]
        att_turned = st.sem("att_turned")
        a_hi_done = st.sem("a_hi_done")
        a_lo_done = st.sem("a_lo_done")
        g_ready = [st.sem(f"g_ready{p}") for p in range(2)]
        y_done = st.sem("y_done")
        gated_done = st.sem("gated_done")
        mixed_done = st.sem("mixed_done")
        mix_hi_done = st.sem("mix_hi_done")
        mix_lo_done = st.sem("mix_lo_done")
        out_done = st.sem("out_done")
        x_ready = [st.sem(f"x_ready{p}") for p in range(2)]
        x2_done = st.sem("x2_done")
        ssq_done = st.sem("ssq_done")
        mean_done = st.sem("mean_done")
        root_done = st.sem("root_done")
        rstd_done = st.sem("rstd_done")
        h_done = st.sem("h_done")
        x2_out = [st.sem(f"x2_out{p}") for p in range(2)]
        h_out = st.sem("h_out")
        block = st.block()
        NBLK = SEQ // MB

        @block.sync
        def _(sp):
            sp.dma_start(g_row[:], norm_ffn.partition_broadcast(P)).then_inc(const_in, 16)
            sp.dma_start(idt[:], ident).then_inc(const_in, 16)
            def load_att(i):
                for t in range(2):
                    sp.dma_start(att_in[t][:], att[ds(i * MB + t * P, P), :]).then_inc(att_ready[t], 16)

            load_att(0)
            for s in range(OUT_SLABS):
                if s >= 2:
                    sp.wait_ge(w_lo_done, s - 1)
                sp.dma_start(w_raw[s % 2][:], w_mix[s]).then_inc(w_in[s % 2], 16)

            with sp.Fori(0, NBLK) as i:
                sp.wait_ge(att_turned, i * 4 + 4)
                hold(sp, held)
                nxt = i * MB + MB
                for t in range(2):
                    sp.dma_start(att_in[t][:], att[ds(nxt + t * P, P), :]).then_inc(att_ready[t], 16)
                for o in range(KD):
                    sp.wait_ge(gated_done, i * KD + o + 1)
                    hold(sp, held)
                    for br in range(2):
                        sp.dma_start(g_in[o % 2][:, br * MB:(br + 1) * MB],
                                     gates[br * KD + o, :, ds(i * MB, MB)]).then_inc(g_ready[o % 2], 16)
                for t in range(2):
                    sp.wait_ge(x2_out[t], i * 16 + 16)
                    hold(sp, held)
                    sp.wait_ge(h_done, i * 2 + t + 1)
                    hold(sp, held)
                    sp.dma_start(x_t[t][:], x[ds(i * MB + t * P, P), :]).then_inc(x_ready[t], 16)
            for t in range(2):
                sp.wait_ge(x2_out[t], 16 * NBLK + 16)
                sp.wait_ge(att_ready[t], 16 * (NBLK + 1))
            sp.wait_ge(h_out, 16 * NT + 16)

        @block.gpsimd
        def _(pool):
            with pool.Fori(0, NBLK) as i:
                for o in range(KD):
                    pool.wait_ge(gated_done, i * KD + o + 3)
                    pool.wait_ge(mix_lo_done, i * KD + o + 1)
                    pool.tensor_tensor(mixed[o % 2][:], gated[o % 2][:, :MB], gated[o % 2][:, MB:],
                                       ALU.add).then_inc(mixed_done, 1)

        @block.scalar
        def _(act):
            act.sem_inc(h_out, 16)
            for t in range(2):
                act.sem_inc(x2_out[t], 16)

            def split(first):
                for s in range(first, first + KD):
                    act.wait_ge(w_in[s % 2], 16 * (s // 2 + 1))
                    act.activation(w_hi[:, s, :], w_raw[s % 2][:], ACT.Copy).then_inc(w_hi_done, 1)

            def att_hi(i):
                for t in range(2):
                    for b in range(2):
                        act.wait_ge(att_turned, i * 4 + 2 * t + b + 1)
                        act.activation(aT_hi[:, 4 * b:4 * b + 4, t * P:(t + 1) * P],
                                       t_ps[b][:].rearrange("p (k t) -> p k t", k=4), ACT.Copy).then_inc(a_hi_done, 1)

            split(0)
            att_hi(0)
            split(KD)
            with act.Fori(0, NBLK) as i:
                for o in range(KD):
                    act.wait_ge(mixed_done, i * KD + o + 3)
                    if o == 0:
                        act.wait_ge(out_done, i * 2 + 2)
                    act.activation(mix_hi[:, o, :], mixed[o % 2][:], ACT.Copy).then_inc(mix_hi_done, 1)
                att_hi(i + 1)
                for t in range(2):
                    act.wait_ge(x2_done, i * 4 + 2 * t + 6)
                    act.activation(junk[:], x_t[t][:], ACT.Square, accum_out=stat[t][:, 0:1]).then_inc(ssq_done, 1)
                    root(act, stat[t], i * 2 + t, mean_done, root_done)
                    act.dma_start(x2[ds(i * MB + t * P, P), :], x_t[t][:]).then_inc(x2_out[t], 16)
                    act.wait_ge(h_done, i * 2 + t + 3)
                    act.dma_start(h2[ds(i * MB + t * P, P), :], h_t[:]).then_inc(h_out, 16)

        @block.vector
        def _(dve):
            def split(first):
                for s in range(first, first + KD):
                    dve.wait_ge(w_hi_done, s + 1)
                    dve.tensor_tensor(w_lo[:, s, :], w_raw[s % 2][:], w_hi[:, s, :],
                                      ALU.subtract).then_inc(w_lo_done, 1)

            dve.wait_ge(const_in, 32)

            def att_lo(i):
                for t in range(2):
                    for b in range(2):
                        dve.wait_ge(a_hi_done, i * 4 + 2 * t + b + 1)
                        where = (slice(None), slice(4 * b, 4 * b + 4), slice(t * P, (t + 1) * P))
                        dve.tensor_tensor(aT_lo[where], t_ps[b][:].rearrange("p (k t) -> p k t", k=4),
                                          aT_hi[where], ALU.subtract).then_inc(a_lo_done, 1)

            def gate(i, o):
                dve.wait_ge(g_ready[o % 2], i * (KD // 2 * 32) + (o // 2 + 1) * 32)
                dve.wait_ge(y_done, i * KD + o + 1)
                dve.wait_ge(mixed_done, i * KD + o + 1)
                dve.tensor_tensor(gated[o % 2][:], y_ps[o % 2][:].rearrange("p a t -> p (a t)"), g_in[o % 2][:],
                                  ALU.mult).then_inc(gated_done, 1)

            split(0)
            att_lo(0)
            split(KD)
            with dve.Fori(0, NBLK) as i:
                gate(i, 0)
                for o in range(KD):
                    if o + 1 < KD:
                        gate(i, o + 1)
                    dve.wait_ge(mix_hi_done, i * KD + o + 1)
                    dve.tensor_tensor(mix_lo[:, o, :], mixed[o % 2][:], mix_hi[:, o, :],
                                      ALU.subtract).then_inc(mix_lo_done, 1)
                att_lo(i + 1)
                for t in range(2):
                    dve.wait_ge(x_ready[t], i * 16 + 16)
                    dve.wait_ge(out_done, i * 2 + t + 3)
                    for b in range(2):
                        cols = slice(b * NB, (b + 1) * NB)
                        dve.tensor_tensor(x_t[t][:, cols], o_ps[t][b][:], x_t[t][:, cols], ALU.add).then_inc(x2_done, 1)
                    mean_square(dve, stat[t], i * 2 + t, ssq_done, mean_done)
                    inverse_rms(dve, stat[t], i * 2 + t, root_done, rstd_done)
                    dve.wait_ge(h_out, (i * 2 + t) * 16 + 16)
                    dve.scalar_tensor_tensor(h_t[:], x_t[t][:], stat[t][:, 4:5], g_row[:],
                                             ALU.mult, ALU.mult).then_inc(h_done, 1)

        @block.tensor
        def _(pe):
            pe.sem_inc(a_lo_done, 2)
            pe.sem_inc(gated_done, 2)
            pe.sem_inc(mixed_done, 2)
            pe.sem_inc(mix_lo_done, 2)
            pe.sem_inc(h_done, 2)
            pe.sem_inc(x2_done, 4)
            pe.sem_inc(out_done, 2)
            pe.wait_ge(const_in, 32)

            def turn_att(i):
                for t in range(2):
                    pe.wait_ge(att_ready[t], i * 16 + 16)
                    for b in range(2):
                        pe.wait_ge(a_lo_done, i * 4 + 2 * t + b + 1)
                        for k in range(4):
                            last = pe.transpose(t_ps[b][:, k * P:(k + 1) * P],
                                                att_in[t][:, (4 * b + k) * P:(4 * b + k + 1) * P], idt[:])
                        last.then_inc(att_turned, 1)

            turn_att(0)
            pe.wait_ge(w_lo_done, KD)
            with pe.Fori(0, NBLK) as i:
                pe.wait_ge(a_lo_done, i * 4 + 6)
                for o in range(KD):
                    pe.wait_ge(gated_done, i * KD + o + 1)
                    cols = slice(o * P, (o + 1) * P)
                    for br in range(2):
                        for k in range(4 * br, 4 * br + 4):
                            y = y_ps[o % 2][:, br, :]
                            pe.matmul(y, w_hi[:, k, cols], aT_hi[:, k, :], start=(k % 4 == 0), stop=False)
                            pe.matmul(y, w_hi[:, k, cols], aT_lo[:, k, :], start=False, stop=False)
                            last = pe.matmul(y, w_lo[:, k, cols], aT_hi[:, k, :], start=False, stop=(k % 4 == 3))
                    last.then_inc(y_done, 1)
                turn_att(i + 1)
                pe.wait_ge(w_lo_done, OUT_SLABS)
                for t in range(2):
                    pe.wait_ge(x2_done, i * 4 + 2 * t + 2)
                    tok = slice(t * P, (t + 1) * P)
                    for k in range(KD):
                        if t == 0:
                            pe.wait_ge(mix_lo_done, i * KD + k + 3)
                        for m, w, first, end in ((mix_hi, w_hi, k == 0, False), (mix_hi, w_lo, False, False),
                                                 (mix_lo, w_hi, False, k == KD - 1)):
                            for b in range(2):
                                last = pe.matmul(o_ps[t][b][:], m[:, k, tok], w[:, KD + k, b * NB:(b + 1) * NB],
                                                 start=first, stop=end)
                    last.then_inc(out_done, 1)


GROUPS = 4
PER_GROUP = 8
EXPERTS = GROUPS * PER_GROUP
LOGITS = GROUPS + EXPERTS
MAX_TILES = 2 * SEQ // P + EXPERTS
BIG = 3e38


FRONT = 2


class Routes:

    def __init__(self, st):
        self.slot = [st.sb(f"slot{k}", [P, NT], U32) for k in range(2)]
        self.weight = [st.sb(f"weight{k}", [P, NT]) for k in range(2)]
        self.token = st.sb("token", [P, MAX_TILES + 2], U32)
        self.first = st.sb("first", [1, EXPERTS], I32)
        self.last = st.sb("last", [1, EXPERTS], I32)


def route(nc, h2, w_router, b_router, ident, strict_upper, token_ids, table, routes):
    with Stage(nc, "rt") as st:
        h_in = [st.sb(f"h_in{p}", [P, D]) for p in range(2)]
        hT = [st.sb(f"hT{p}", [P, KD, P]) for p in range(2)]
        w_r = st.sb("w_r", [P, KD, LOGITS])
        b_r = st.sb("b_r", [P, LOGITS])
        idt = st.sb("idt", [P, P])
        upper = st.sb("upper", [P, P])
        ones = st.sb("ones", [P, P])
        ids = st.sb("ids", [P, NT])
        logit = st.sb("logit", [P, NT, LOGITS])
        t_ps = [[st.ps(f"t_ps{p}{b}", [P, NB]) for b in range(2)] for p in range(2)]
        l_ps = [st.ps(f"l_ps{p}", [P, NB]) for p in range(2)]
        c_ps = [st.ps(f"c_ps{b}", [P, NT, EXPERTS]) for b in range(2)]

        held = st.sem("held")
        const_in = st.sem("const_in")
        h_ready = [st.sem(f"h_ready{p}") for p in range(2)]
        turned = st.sem("turned")
        copied = st.sem("copied")
        logit_mm = st.sem("logit_mm")
        logit_done = st.sem("logit_done")
        exp_asked = st.sem("exp_asked")
        exp_done = st.sem("exp_done")
        count_asked = st.sem("count_asked")
        counted = st.sem("counted")
        routed = st.sem("routed")
        zeroed = st.sem("zeroed")
        scattered = st.sem("scattered")
        table_in = st.sem("table_in")
        table_turned = st.sem("table_turned")
        step = st.sem("step")
        block = st.block()

        g4 = st.sb("g4", [P, NT, GROUPS])
        g_hot = st.sb("g_hot", [P, NT, GROUPS])
        g_work = st.sb("g_work", [P, NT, GROUPS])
        g_exp = st.sb("g_exp", [P, NT, GROUPS])
        prio4 = st.sb("prio4", [P, NT, GROUPS])
        prio8 = st.sb("prio8", [P, NT, PER_GROUP])
        wide = st.sb("wide", [P, NT, GROUPS, PER_GROUP])
        inner = st.sb("inner", [P, NT, PER_GROUP])
        inner2 = st.sb("inner2", [P, NT, PER_GROUP])
        e8 = st.sb("e8", [P, NT, PER_GROUP])
        hot8 = [st.sb(f"hot8{k}", [P, NT, PER_GROUP]) for k in range(2)]
        hot = [st.sb(f"hot{k}", [P, NT, EXPERTS]) for k in range(2)]
        both = st.sb("both", [P, NT, EXPERTS])
        rank = st.sb("rank", [P, NT, EXPERTS])
        base = st.sb("base", [P, NT + 1, EXPERTS])
        picked = st.sb("picked", [P, NT, EXPERTS])
        top = st.sb("top", [P, 8, NT])
        slot_f = st.sb("slot_f", [P, 2, NT])
        place = [st.sb(f"place{k}", [P, NT], U32) for k in range(2)]
        cnt_i = st.sb("cnt_i", [P, EXPERTS], I32)
        tiles_f = st.sb("tiles_f", [P, EXPERTS])
        ends = st.sb("ends", [P, EXPERTS])
        starts = st.sb("starts", [P, EXPERTS])
        one_row = st.sb("one_row", [P, EXPERTS])
        zero = st.sb("zero", [MAX_TILES, P])
        tab = st.sb("tab", [MAX_TILES, P])

        @block.sync
        def _(sp):
            sp.dma_start(w_r[:], w_router.rearrange("p (k n) -> p k n", k=KD)).then_inc(const_in, 16)
            sp.dma_start(b_r[:], b_router.partition_broadcast(P)).then_inc(const_in, 16)
            sp.dma_start(idt[:], ident).then_inc(const_in, 16)
            sp.dma_start(upper[:], strict_upper).then_inc(const_in, 16)
            sp.dma_start(ids[:], token_ids).then_inc(const_in, 16)
            for p in range(2):
                sp.dma_start(h_in[p][:], h2[p * P:(p + 1) * P, :]).then_inc(h_ready[p], 16)
            with sp.Fori(1, NT // 2) as i:
                for p in range(2):
                    sp.wait_ge(turned, i * 2 + p - 1)
                    hold(sp, held)
                    sp.dma_start(h_in[p][:], h2[ds((i * 2 + p) * P, P), :]).then_inc(h_ready[p], 16)

        @block.gpsimd
        def _(pool):
            pool.memset(zero[:], 0.0).then_inc(zeroed, 1)
            pool.memset(ones[:], 1.0).then_inc(zeroed, 1)
            pool.wait_ge(zeroed, 2)
            pool.dma_start(table.rearrange("(t p) a -> t (p a)", p=P), zero[:]).then_inc(scattered, 16)
            pool.wait_ge(scattered, 16)
            pool.wait_ge(const_in, 80)
            pool.wait_ge(routed, 1)
            for t in range(NT):
                for k in range(2):
                    pool.indirect_dma_start(
                        out=table, out_offset=bass.IndirectOffsetOnAxis(ap=place[k][:, t:t + 1], axis=0),
                        in_=ids[:, t:t + 1], in_offset=None).then_inc(scattered, 16)
            pool.wait_ge(scattered, 16 * (2 * NT + 1))
            pool.dma_start(tab[:], table.rearrange("(t p) a -> t (p a)", p=P)).then_inc(table_in, 16)

        @block.scalar
        def _(act):
            with act.Fori(0, NT // 2) as i:
                for p in range(2):
                    act.wait_ge(turned, i * 2 + p + 1)
                    for b in range(2):
                        act.activation(hT[p][:, 4 * b:4 * b + 4, :], t_ps[p][b][:].rearrange("p (k t) -> p k t", k=4),
                                       ACT.Copy).then_inc(copied, 1)
            act.wait_ge(exp_asked, 1)
            act.activation(g_exp[:], g4[:], ACT.Exp).then_inc(exp_done, 1)
            act.wait_ge(exp_asked, 2)
            act.activation(top[:, 4, :], top[:, 3, :], ACT.Exp).then_inc(exp_done, 1)

        @block.tensor
        def _(pe):
            pe.sem_inc(logit_done, 2)
            pe.wait_ge(const_in, 80)
            with pe.Fori(0, NT // 2) as i:
                for p in range(2):
                    pe.wait_ge(h_ready[p], i * 16 + 16)
                    for k in range(KD):
                        last = pe.transpose(t_ps[p][k // 4][:, (k % 4) * P:(k % 4 + 1) * P],
                                            h_in[p][:, k * P:(k + 1) * P], idt[:])
                    last.then_inc(turned, 1)
                for p in range(2):
                    pe.wait_ge(copied, i * 4 + 2 * p + 2)
                    pe.wait_ge(logit_done, i * 2 + p + 1)
                    for k in range(KD):
                        last = pe.matmul(l_ps[p][:, :LOGITS], hT[p][:, k, :], w_r[:, k, :],
                                         start=(k == 0), stop=(k == KD - 1))
                    last.then_inc(logit_mm, 1)
            pe.wait_ge(count_asked, 1)
            flat = both[:].rearrange("p t e -> p (t e)")
            pe.matmul(c_ps[0][:].rearrange("p t e -> p (t e)"), upper[:], flat, start=True, stop=True)
            pe.wait_ge(zeroed, 2)
            pe.matmul(c_ps[1][:].rearrange("p t e -> p (t e)"), ones[:], flat,
                      start=True, stop=True).then_inc(counted, 1)
            pe.wait_ge(table_in, 16)
            pe.transpose(l_ps[0][:, :MAX_TILES], tab[:], idt[:MAX_TILES, :MAX_TILES]).then_inc(table_turned, 1)

        @block.vector
        def _(dve):
            n = [0]

            def then(ins, sem=None):
                n[0] += 1
                ins.then_inc(step, 1)
                dve.wait_ge(step, n[0])

            def over(ap, m):
                return ap.unsqueeze(2).broadcast_to([P, NT, m])

            dve.wait_ge(const_in, 80)
            with dve.Fori(0, NT // 2) as i:
                for p in range(2):
                    dve.wait_ge(logit_mm, i * 2 + p + 1)
                    hold(dve, held)
                    dve.tensor_tensor(logit[:, ds(i * 2 + p, 1), :].rearrange("p a n -> p (a n)"),
                                      l_ps[p][:, :LOGITS], b_r[:], ALU.add).then_inc(logit_done, 1)
            for g in range(GROUPS):
                then(dve.memset(prio4[:, :, g], float(GROUPS - g)))
            for e in range(PER_GROUP):
                then(dve.memset(prio8[:, :, e], float(PER_GROUP - e)))
            then(dve.memset(one_row[:], 1.0))
            dve.wait_ge(logit_done, NT + 2)
            g_logit = logit[:, :, :GROUPS]
            e_logit = logit[:, :, GROUPS:].rearrange("p t (g e) -> p t g e", g=GROUPS)

            def first_of(hot_out, value, high, prio, work, slot):
                m = value.shape[2]
                then(dve.tensor_tensor(work, value, over(high, m), ALU.is_equal))
                then(dve.tensor_tensor(work, work, prio, ALU.mult))
                then(dve.tensor_reduce(top[:, slot, :], work, AX_X, ALU.max))
                then(dve.tensor_tensor(hot_out, work, over(top[:, slot, :], m), ALU.is_equal))

            then(dve.tensor_reduce(top[:, 0, :], g_logit, AX_X, ALU.max))
            dve.tensor_tensor(g4[:], g_logit, over(top[:, 0, :], GROUPS), ALU.subtract).then_inc(exp_asked, 1)
            first_of(g_hot[:], g_logit, top[:, 0, :], prio4[:], g_work[:], 5)
            then(dve.tensor_tensor(wide[:], e_logit,
                                   g_hot[:].unsqueeze(3).broadcast_to([P, NT, GROUPS, PER_GROUP]), ALU.mult))
            then(dve.tensor_reduce(inner[:], wide[:].rearrange("p t g e -> p t e g"), AX_X, ALU.add))
            then(dve.tensor_reduce(top[:, 1, :], inner[:], AX_X, ALU.max))
            first_of(hot8[0][:], inner[:], top[:, 1, :], prio8[:], e8[:], 5)
            then(dve.scalar_tensor_tensor(inner2[:], hot8[0][:], -BIG, inner[:], ALU.mult, ALU.add))
            then(dve.tensor_reduce(top[:, 2, :], inner2[:], AX_X, ALU.max))
            first_of(hot8[1][:], inner2[:], top[:, 2, :], prio8[:], e8[:], 5)
            then(dve.tensor_tensor(top[:, 3, :], top[:, 2, :], top[:, 1, :], ALU.subtract))
            dve.sem_inc(exp_asked, 1)
            for k in range(2):
                then(dve.tensor_tensor(hot[k][:].rearrange("p t (g e) -> p t g e", g=GROUPS),
                                       g_hot[:].unsqueeze(3).broadcast_to([P, NT, GROUPS, PER_GROUP]),
                                       hot8[k][:].unsqueeze(2).broadcast_to([P, NT, GROUPS, PER_GROUP]), ALU.mult))
            dve.tensor_tensor(both[:], hot[0][:], hot[1][:], ALU.add).then_inc(count_asked, 1)
            dve.wait_ge(exp_done, 2)
            then(dve.tensor_reduce(top[:, 5, :], g_exp[:], AX_X, ALU.add))
            then(dve.scalar_tensor_tensor(top[:, 6, :], top[:, 4, :], 1.0, top[:, 5, :], ALU.add, ALU.mult))
            then(dve.reciprocal(routes.weight[0][:], top[:, 6, :]))
            then(dve.tensor_tensor(routes.weight[1][:], routes.weight[0][:], top[:, 4, :], ALU.mult))
            dve.wait_ge(counted, 1)
            then(dve.memset(base[:, 0, :], 0.0))
            for t in range(NT):
                then(dve.tensor_tensor(base[:, t + 1, :], c_ps[1][:, t, :], base[:, t, :], ALU.add))
            then(dve.tensor_tensor(rank[:], c_ps[0][:], base[:, :NT, :], ALU.add))
            then(dve.tensor_scalar(cnt_i[:], base[:, NT, :], float(P - 1), None, ALU.add))
            then(dve.tensor_single_scalar(cnt_i[:], cnt_i[:], 7, ALU.arith_shift_right))
            then(dve.tensor_scalar(tiles_f[:], cnt_i[:], 1.0, None, ALU.max))
            then(dve.tensor_tensor_scan(ends[:], one_row[:], tiles_f[:], 0.0, ALU.mult, ALU.add))
            then(dve.tensor_tensor(starts[:], ends[:], tiles_f[:], ALU.subtract))
            then(dve.tensor_copy(routes.first[:], starts[0:1, :]))
            then(dve.tensor_scalar(routes.last[:], ends[0:1, :], -1.0, None, ALU.add))
            then(dve.tensor_scalar(starts[:], starts[:], float(P), None, ALU.mult))
            then(dve.tensor_tensor(rank[:], rank[:],
                                   starts[:].unsqueeze(1).broadcast_to([P, NT, EXPERTS]), ALU.add))
            for k in range(2):
                then(dve.tensor_tensor(picked[:], rank[:], hot[k][:], ALU.mult))
                then(dve.tensor_reduce(slot_f[:, k, :], picked[:], AX_X, ALU.add))
                then(dve.tensor_copy(place[k][:], slot_f[:, k, :]))
                then(dve.tensor_scalar(routes.slot[k][:], slot_f[:, k, :], float(FRONT * P), None, ALU.add))
            dve.sem_inc(routed, 1)
            dve.wait_ge(table_turned, 1)
            then(dve.memset(routes.token[:, MAX_TILES:], 0))
            then(dve.tensor_copy(routes.token[:, :MAX_TILES], l_ps[0][:, :MAX_TILES]))


DE = 512
KE = DE // P
CHUNKS = 4


def experts(nc, h2, w_gate, w_up, w_down, ident, ys, routes):
    with Stage(nc, "ex") as st:
        raw = [[st.sb(f"raw_{m}{j}", [P, D]) for j in range(CHUNKS)] for m in "gud"]
        wg_hi, wg_lo, wu_hi, wu_lo = (st.sb(n, [P, KD, DE], F32R) for n in ("wg_hi", "wg_lo", "wu_hi", "wu_lo"))
        wd_hi = [st.sb(f"wd_hi{p}", [P, KE, D], F32R) for p in range(2)]
        wd_lo = [st.sb(f"wd_lo{p}", [P, KE, D], F32R) for p in range(2)]
        idt = st.sb("idt", [P, P])
        rows = st.sb("rows", [P, 1], U32)
        x_in = st.sb("x_in", [P, D])
        xT_hi, xT_lo = st.sb("xT_hi", [P, KD, P], F32R), st.sb("xT_lo", [P, KD, P], F32R)
        silu = st.sb("silu", [P, DE])
        a = st.sb("a", [P, DE])
        aT_hi, aT_lo = st.sb("aT_hi", [P, KE, P], F32R), st.sb("aT_lo", [P, KE, P], F32R)
        y = st.sb("y", [P, D])
        g_ps, u_ps, a_ps = (st.ps(n, [P, NB]) for n in ("g_ps", "u_ps", "a_ps"))
        x_ps = [st.ps(f"x_ps{b}", [P, NB]) for b in range(2)]
        y_ps = [st.ps(f"y_ps{b}", [P, NB]) for b in range(2)]

        held = st.sem("held")
        idt_in = st.sem("idt_in")
        raw_in = [[st.sem(f"raw_in_{m}{j}") for j in range(CHUNKS)] for m in "gud"]
        g_hi_done, u_hi_done, d_hi_done = (st.sem(n) for n in ("g_hi_done", "u_hi_done", "d_hi_done"))
        g_lo_done, u_lo_done = st.sem("g_lo_done"), st.sem("u_lo_done")
        d_lo_pool, d_lo_dve = st.sem("d_lo_pool"), st.sem("d_lo_dve")
        rows_ready = st.sem("rows_ready")
        x_ready = st.sem("x_ready")
        x_turned = st.sem("x_turned")
        xT_hi_done, xT_lo_done = st.sem("xT_hi_done"), st.sem("xT_lo_done")
        gate_done, up_done = st.sem("gate_done"), st.sem("up_done")
        silu_done = st.sem("silu_done")
        a_done = st.sem("a_done")
        a_turned = st.sem("a_turned")
        aT_hi_done, aT_lo_done = st.sem("aT_hi_done"), st.sem("aT_lo_done")
        down_done = st.sem("down_done")
        y_done = st.sem("y_done")
        y_stored = st.sem("y_stored")
        block = st.block()

        def slabs(buffer, m, j):
            return buffer[:, 2 * j:2 * j + 2, :].rearrange("p k n -> p (k n)") if m < 2 else buffer[:, j, :]

        def span(eng, e):
            first = eng.value_load(routes.first[0:1, ds(e, 1)], min_val=0, max_val=MAX_TILES - 1)
            last = eng.value_load(routes.last[0:1, ds(e, 1)], min_val=0, max_val=MAX_TILES - 1)
            return first, last

        def last_of_all(eng):
            return eng.value_load(routes.last[0:1, EXPERTS - 1:EXPERTS], min_val=0, max_val=MAX_TILES - 1)

        def over_experts(eng, each):
            with eng.Fori(0, EXPERTS // 2 - 1) as i:
                for p in range(2):
                    each(i * 2 + p, p, True)
            each(EXPERTS - 2, 0, True)
            each(EXPERTS - 1, 1, False)

        @block.sync
        def _(sp):
            def load(e, m, j):
                if m < 2:
                    sp.dma_start(raw[m][j][:].rearrange("p (s n) -> p s n", s=2),
                                 (w_gate, w_up)[m][ds(e, 1), 2 * j * P:(2 * j + 2) * P, :].rearrange(
                                     "a (s p) n -> p (a s) n", p=P)).then_inc(raw_in[m][j], 16)
                else:
                    sp.dma_start(raw[m][j][:], w_down[ds(e, 1), j * P:(j + 1) * P, :].rearrange(
                        "a p n -> (a p) n")).then_inc(raw_in[m][j], 16)

            sp.dma_start(idt[:], ident).then_inc(idt_in, 16)
            for m in range(3):
                for j in range(CHUNKS):
                    load(0, m, j)
            with sp.Fori(1, EXPERTS) as e:
                for m in range(3):
                    for j in range(CHUNKS):
                        if m < 2:
                            sp.wait_ge((g_lo_done, u_lo_done)[m], e * CHUNKS + (j + 1 - CHUNKS))
                        else:
                            sp.wait_ge((d_lo_pool, d_lo_dve)[j // 2], e * 2 + (j % 2 - 1))
                        hold(sp, held)
                        load(e, m, j)

        @block.gpsimd
        def _(pool):
            def gather(n):
                pool.tensor_copy(rows[:], routes.token[:, ds(n, 1)]).then_inc(rows_ready, 1)
                pool.wait_ge(rows_ready, n + 1)
                hold(pool, held)
                pool.indirect_dma_start(out=x_in[:], out_offset=None, in_=h2,
                                        in_offset=bass.IndirectOffsetOnAxis(ap=rows[:, 0:1], axis=0)
                                        ).then_inc(x_ready, 16)

            def step(n):
                pool.wait_ge(x_turned, n + 2)
                gather(n + 2)

            def split_down(e, p):
                for j in range(2):
                    pool.wait_ge(d_hi_done, e * CHUNKS + j + 1)
                    pool.tensor_tensor(wd_lo[p][:, j, :], raw[2][j][:], wd_hi[p][:, j, :],
                                       ALU.subtract).then_inc(d_lo_pool, 1)

            gather(0)
            pool.wait_ge(x_turned, 1)
            gather(1)
            split_down(0, 0)

            def each(e, p, more):
                first, last = span(pool, e)
                with pool.Fori(first, last + 1) as n:
                    step(n)
                if more:
                    split_down(e + 1, 1 - p)

            over_experts(pool, each)
            end = last_of_all(pool) + 1
            pool.wait_ge(x_ready, end * 16 + 32)

        @block.scalar
        def _(act):
            def split(e, m, dst, done):
                for j in range(CHUNKS):
                    act.wait_ge(raw_in[m][j], e * 16 + 16)
                    act.activation(slabs(dst, m, j), raw[m][j][:], ACT.Copy).then_inc(done, 1)

            def store(n):
                act.wait_ge(y_done, n + 1)
                hold(act, held)
                act.dma_start(ys[ds(n * P, P), :], y[:]).then_inc(y_stored, 16)

            def silu_and_aT(n):
                act.wait_ge(gate_done, n + 1)
                act.wait_ge(a_done, n + 1)
                act.activation(silu[:], g_ps[:], ACT.Silu).then_inc(silu_done, 1)
                store(n)
                act.wait_ge(a_turned, n + 1)
                act.activation(aT_hi[:].rearrange("p k t -> p (k t)"), a_ps[:], ACT.Copy).then_inc(aT_hi_done, 1)

            def xT(n):
                act.wait_ge(x_turned, n + 1)
                for b in range(2):
                    act.activation(xT_hi[:, 4 * b:4 * b + 4, :], x_ps[b][:].rearrange("p (k t) -> p k t", k=4),
                                   ACT.Copy).then_inc(xT_hi_done, 1)

            split(0, 0, wg_hi, g_hi_done)
            xT(0)
            split(0, 1, wu_hi, u_hi_done)
            split(0, 2, wd_hi[0], d_hi_done)

            def each(e, p, more):
                first, last = span(act, e)
                with act.If(last > first):
                    with act.Fori(first, last) as n:
                        silu_and_aT(n)
                        xT(n + 1)
                silu_and_aT(last)
                if more:
                    split(e + 1, 0, wg_hi, g_hi_done)
                xT(last + 1)
                if more:
                    split(e + 1, 1, wu_hi, u_hi_done)
                    act.wait_ge(down_done, first + 1)
                    split(e + 1, 2, wd_hi[1 - p], d_hi_done)

            over_experts(act, each)
            end = last_of_all(act) + 1
            act.wait_ge(a_turned, end + 1)
            act.activation(aT_hi[:].rearrange("p k t -> p (k t)"), a_ps[:], ACT.Copy).then_inc(aT_hi_done, 1)
            store(end)
            store(end + 1)
            act.wait_ge(y_stored, end * 16 + 32)
            hold(act, held)

        @block.vector
        def _(dve):
            def split(e, m, hi, lo, hi_done, lo_done):
                for j in range(CHUNKS):
                    dve.wait_ge(hi_done, e * CHUNKS + j + 1)
                    dve.tensor_tensor(slabs(lo, m, j), raw[m][j][:], slabs(hi, m, j),
                                      ALU.subtract).then_inc(lo_done, 1)

            def split_down(e, p):
                for j in range(2, CHUNKS):
                    dve.wait_ge(d_hi_done, e * CHUNKS + j + 1)
                    dve.tensor_tensor(wd_lo[p][:, j, :], raw[2][j][:], wd_hi[p][:, j, :],
                                      ALU.subtract).then_inc(d_lo_dve, 1)

            def aT(n):
                dve.wait_ge(aT_hi_done, n + 1)
                dve.tensor_tensor(aT_lo[:].rearrange("p k t -> p (k t)"), a_ps[:],
                                  aT_hi[:].rearrange("p k t -> p (k t)"), ALU.subtract).then_inc(aT_lo_done, 1)

            def a_and_xT(n):
                dve.wait_ge(up_done, n + 1)
                dve.wait_ge(silu_done, n + 2)
                dve.tensor_tensor(a[:], u_ps[:], silu[:], ALU.mult).then_inc(a_done, 1)
                xT(n + 1)

            def xT(n):
                for b in range(2):
                    dve.wait_ge(xT_hi_done, n * 2 + b + 1)
                    dve.tensor_tensor(xT_lo[:, 4 * b:4 * b + 4, :], x_ps[b][:].rearrange("p (k t) -> p k t", k=4),
                                      xT_hi[:, 4 * b:4 * b + 4, :], ALU.subtract).then_inc(xT_lo_done, 1)

            def y_out(n):
                dve.wait_ge(down_done, n + 1)
                dve.wait_ge(y_stored, n * 16 + 16)
                dve.tensor_copy(y[:, :NB], y_ps[0][:])
                dve.tensor_copy(y[:, NB:], y_ps[1][:]).then_inc(y_done, 1)

            dve.memset(a[:], 0.0).then_inc(a_done, 1)
            dve.memset(y[:], 0.0).then_inc(y_done, 1)
            split(0, 0, wg_hi, wg_lo, g_hi_done, g_lo_done)
            xT(0)
            split(0, 1, wu_hi, wu_lo, u_hi_done, u_lo_done)
            split_down(0, 0)

            def each(e, p, more):
                first, last = span(dve, e)
                with dve.If(last > first):
                    with dve.Fori(first, last) as n:
                        aT(n)
                        a_and_xT(n)
                        y_out(n)
                aT(last)
                if more:
                    split(e + 1, 0, wg_hi, wg_lo, g_hi_done, g_lo_done)
                a_and_xT(last)
                if more:
                    split(e + 1, 1, wu_hi, wu_lo, u_hi_done, u_lo_done)
                y_out(last)
                if more:
                    split_down(e + 1, 1 - p)

            over_experts(dve, each)
            end = last_of_all(dve) + 1
            aT(end)
            y_out(end)

        @block.tensor
        def _(pe):
            def times(out, xT_parts, w_parts, chunk, cols):
                for k in chunk:
                    for c, (x, w) in enumerate(((0, 0), (1, 0), (0, 1))):
                        last = pe.matmul(out, xT_parts[x][:, k, :], w_parts[w][:, k, cols],
                                         start=(k == 0 and c == 0), stop=(k == xT_parts[2] - 1 and c == 2))
                return last

            xT = (xT_hi, xT_lo, KD)
            aT = (aT_hi, aT_lo, KE)

            def turn_a():
                for k in range(KE):
                    last = pe.transpose(a_ps[:, k * P:(k + 1) * P], a[:, k * P:(k + 1) * P], idt[:])
                last.then_inc(a_turned, 1)

            def turn_x(n):
                pe.wait_ge(x_ready, n * 16 + 16)
                for k in range(KD):
                    last = pe.transpose(x_ps[k // 4][:, (k % 4) * P:(k % 4 + 1) * P],
                                        x_in[:, k * P:(k + 1) * P], idt[:])
                last.then_inc(x_turned, 1)

            def down(n, p):
                pe.wait_ge(aT_lo_done, n + 1)
                pe.wait_ge(y_done, n + 1)
                for b in range(2):
                    last = times(y_ps[b][:], aT, (wd_hi[p], wd_lo[p]), range(KE), slice(b * NB, (b + 1) * NB))
                last.then_inc(down_done, 1)

            def step(n, p, e=None):
                pe.wait_ge(xT_lo_done, n * 2 + 2)
                pe.wait_ge(silu_done, n + 1)
                for j in range(CHUNKS):
                    if e is not None:
                        pe.wait_ge(g_lo_done, e * CHUNKS + j + 1)
                    last = times(g_ps[:], xT, (wg_hi, wg_lo), range(2 * j, 2 * j + 2), slice(0, DE))
                last.then_inc(gate_done, 1)
                pe.wait_ge(a_done, n + 1)
                turn_a()
                for j in range(CHUNKS):
                    if e is not None:
                        pe.wait_ge(u_lo_done, e * CHUNKS + j + 1)
                    last = times(u_ps[:], xT, (wu_hi, wu_lo), range(2 * j, 2 * j + 2), slice(0, DE))
                last.then_inc(up_done, 1)
                turn_x(n + 1)
                down(n, p)

            pe.sem_inc(silu_done, 1)
            pe.wait_ge(idt_in, 16)
            turn_x(0)

            def each(e, p, first_of_all=False):
                first, last = span(pe, e)
                if first_of_all:
                    pe.wait_ge(d_lo_pool, 2)
                    pe.wait_ge(d_lo_dve, 2)
                    step(first, p, e)
                else:
                    step(first, 1 - p, e)
                    pe.wait_ge(d_lo_pool, e * 2 + 2)
                    pe.wait_ge(d_lo_dve, e * 2 + 2)
                with pe.If(last > first):
                    with pe.Fori(first + 1, last + 1) as n:
                        step(n, p)

            each(0, 0, first_of_all=True)
            each(1, 1)
            with pe.Fori(1, EXPERTS // 2) as i:
                for p in range(2):
                    each(i * 2 + p, p)
            end = last_of_all(pe) + 1
            pe.wait_ge(a_done, end + 1)
            turn_a()
            down(end, 1)


def combine(nc, x2, ys, norm_final, out, routes):
    with Stage(nc, "cb") as st:
        BUFS = 6
        x_in = [st.sb(f"x_in{p}", [P, D]) for p in range(BUFS)]
        y_in = [[st.sb(f"y_in{p}{k}", [P, D]) for k in range(2)] for p in range(BUFS)]
        done = [st.sb(f"done{p}", [P, D]) for p in range(2)]
        junk = [st.sb(f"junk{p}", [P, D], BF16) for p in range(2)]
        stat = [st.sb(f"stat{p}", [P, 8]) for p in range(2)]
        g_row = st.sb("g_row", [P, D])
        const_in = st.sem("const_in")
        x_ready = [st.sem(f"x_ready{p}") for p in range(BUFS)]
        y_ready = [st.sem(f"y_ready{p}") for p in range(BUFS)]
        summed = st.sem("summed")
        ssq_done, mean_done, root_done, rstd_done = (
            st.sem(n) for n in ("ssq_done", "mean_done", "root_done", "rstd_done"))
        normed = st.sem("normed")
        stored = [st.sem(f"stored{p}") for p in range(2)]
        block = st.block()

        @block.sync
        def _(sp):
            sp.dma_start(g_row[:], norm_final.partition_broadcast(P)).then_inc(const_in, 16)

            def load(t):
                sp.dma_start(x_in[t % BUFS][:], x2[t * P:(t + 1) * P, :]).then_inc(x_ready[t % BUFS], 16)

            for t in range(BUFS):
                load(t)
            for t in range(NT):
                sp.wait_ge(normed, t + 1)
                sp.dma_start(out[t * P:(t + 1) * P, :], done[t % 2][:]).then_inc(stored[t % 2], 16)
                if t + BUFS < NT:
                    load(t + BUFS)
            for p in range(2):
                sp.wait_ge(stored[p], 16 * (NT // 2))

        @block.gpsimd
        def _(pool):
            def gather(t):
                for k in range(2):
                    pool.indirect_dma_start(
                        out=y_in[t % BUFS][k][:], out_offset=None, in_=ys,
                        in_offset=bass.IndirectOffsetOnAxis(ap=routes.slot[k][:, t:t + 1], axis=0)
                    ).then_inc(y_ready[t % BUFS], 16)

            for t in range(BUFS):
                gather(t)
            for t in range(NT - BUFS):
                pool.wait_ge(summed, 2 * t + 2)
                gather(t + BUFS)

        @block.scalar
        def _(act):
            for t in range(NT):
                p = t % 2
                act.wait_ge(summed, 2 * t + 2)
                act.activation(junk[p][:], x_in[t % BUFS][:], ACT.Square, accum_out=stat[p][:, 0:1]).then_inc(ssq_done, 1)
                root(act, stat[p], t, mean_done, root_done)

        @block.vector
        def _(dve):
            def add(t):
                p = t % 2
                dve.wait_ge(x_ready[t % BUFS], 16 * (t // BUFS + 1))
                dve.wait_ge(y_ready[t % BUFS], 32 * (t // BUFS + 1))
                for k in range(2):
                    dve.scalar_tensor_tensor(x_in[t % BUFS][:], y_in[t % BUFS][k][:], routes.weight[k][:, t:t + 1], x_in[t % BUFS][:],
                                             ALU.mult, ALU.add).then_inc(summed, 1)
                    dve.wait_ge(summed, 2 * t + k + 1)

            dve.wait_ge(const_in, 16)
            add(0)
            for t in range(NT):
                p = t % 2
                if t + 1 < NT:
                    add(t + 1)
                mean_square(dve, stat[p], t, ssq_done, mean_done)
                inverse_rms(dve, stat[p], t, root_done, rstd_done)
                if t >= 2:
                    dve.wait_ge(stored[p], 16 * (t // 2))
                dve.scalar_tensor_tensor(done[p][:], x_in[t % BUFS][:], stat[p][:, 4:5], g_row[:],
                                         ALU.mult, ALU.mult).then_inc(normed, 1)


def feature_columns():
    a_q, a_k, a_v, b_q, b_k, b_v = 0, 512, 640, 768, 1280, 1792
    spans = [(b_q, 512), (b_k, 512), (b_v, 512), (a_q, 512), (a_k, 128), (a_v, 128)]
    return np.concatenate([np.arange(s, s + n) for s, n in spans])


def layout(x, norm_mix, w_in, w_branch_gate, b_branch_gate):
    w = np.concatenate([w_in[0][:, feature_columns()], w_branch_gate[0]], axis=1)
    tiles = w.shape[1] // P
    return {
        "x": x.reshape(SEQ, D),
        "norm_mix": norm_mix.reshape(D),
        "w_feat": np.ascontiguousarray(w.reshape(KD, P, tiles, P).transpose(2, 1, 0, 3).reshape(tiles, P, D)),
        "gate_bias": np.ascontiguousarray(b_branch_gate.reshape(GATE_TILES, P).T),
        "ident": np.eye(P, dtype=np.float32),
        **rope_tables(),
    }


def band_b(rel_bias):
    q, k = np.arange(P)[:, None], np.arange(5 * P)[None, :] - 4 * P
    idx = np.clip(q - k, -MAX_REL, MAX_REL) + MAX_REL
    chunks = q // CHUNK - k // CHUNK
    rows = rel_bias[0][:, idx]
    rows = np.where((chunks >= 0) & (chunks <= 8), rows, np.float32(NEG))
    return np.ascontiguousarray(np.concatenate([rows, rows[-1:]]).reshape(-1, 5 * P))


def band_a():
    q, k = np.arange(P)[:, None], np.arange(2 * P)[None, :] - P
    chunks = q // CHUNK - k // CHUNK
    return np.where((chunks >= 0) & (chunks <= 1), np.float32(0), np.float32(NEG))


def rope_tables():
    inv = (10000.0 ** (-np.arange(DH // 2) / (DH // 2))).astype(np.float32)
    angle = inv[np.arange(P) % (DH // 2), None] * np.arange(SEQ, dtype=np.float32)
    sign = np.where(np.arange(P) % DH < DH // 2, -1.0, 1.0)[:, None]
    return {"rope_cos": np.cos(angle.astype(np.float64)).astype(np.float32),
            "rope_sin": (sign * np.sin(angle.astype(np.float64))).astype(np.float32)}


def mix_slabs(w_o_a, w_o_b, w_out):
    return np.ascontiguousarray(np.concatenate([w_o_a[0], w_o_b[0], w_out[0]]).reshape(OUT_SLABS, P, D))


def router_layout(w_router_group, b_router_group, w_router_expert, b_router_expert):
    w = np.concatenate([w_router_group[0], w_router_expert[0]], axis=1)
    return {"w_router": np.ascontiguousarray(w.reshape(KD, P, LOGITS).transpose(1, 0, 2).reshape(P, KD * LOGITS)),
            "b_router": np.concatenate([b_router_group[0], b_router_expert[0]]),
            "strict_upper": np.triu(np.ones((P, P), np.float32), 1),
            "token_ids": np.ascontiguousarray(np.arange(SEQ, dtype=np.float32).reshape(NT, P).T)}


def encoder_block(nc, x, norm_mix, w_feat, gate_bias, rope_cos, rope_sin, ident, band, mask, sinks, w_mix,
                  norm_ffn, w_router, b_router, strict_upper, token_ids, w_exp_gate, w_exp_up, w_exp_down,
                  norm_final, out):
    def scratch(name, shape):
        return nc.dram_tensor(f"scratch_{name}", shape, F32, kind="Internal").ap()

    feat = scratch("feat", (COPY_TILES, P, SEQ))
    rotated = scratch("rotated", (ROPE_TILES * P, SEQ))
    gates = scratch("gates", (GATE_TILES, P, SEQ))
    att = scratch("att", (SEQ + MB, D))
    x2, h2 = scratch("x2", (SEQ, D)), scratch("h2", (SEQ, D))
    table = scratch("table", (MAX_TILES * P, 1))
    ys = scratch("ys", ((MAX_TILES + FRONT) * P, D))
    sure = (FRONT + 2 * SEQ // P) * P

    project(nc, x, norm_mix, w_feat, gate_bias, rope_cos, rope_sin, ident, feat, rotated, gates)
    rows = feat.rearrange("a p n -> (a p) n")
    attend_b(nc, rows, band, ident, att)
    attend_a(nc, rows, rotated, mask, sinks, ident, att, (att[SEQ:, :], ys[sure:, :]))
    merge(nc, x, att, gates, w_mix, norm_ffn, ident, x2, h2)
    with Stage(nc, "routes") as st:
        routes = Routes(st)
        route(nc, h2, w_router, b_router, ident, strict_upper, token_ids, table, routes)
        experts(nc, h2, w_exp_gate, w_exp_up, w_exp_down, ident, ys, routes)
        combine(nc, x2, ys, norm_final, out, routes)


def kernel(x, norm_mix, w_in, attn_sinks, rel_bias, w_o_a, w_o_b, w_branch_gate, b_branch_gate, w_out, norm_ffn,
           w_router_group, b_router_group, w_router_expert, b_router_expert, w_exp_gate, w_exp_up, w_exp_down,
           norm_final):
    import concourse.bacc as _bacc
    from concourse.bass_utils import run_bass_kernel_spmd as _run

    (x, norm_mix, w_in, attn_sinks, rel_bias, w_o_a, w_o_b, w_branch_gate, b_branch_gate, w_out, norm_ffn,
     w_router_group, b_router_group, w_router_expert, b_router_expert, w_exp_gate, w_exp_up, w_exp_down,
     norm_final) = (np.asarray(a) for a in (
         x, norm_mix, w_in, attn_sinks, rel_bias, w_o_a, w_o_b, w_branch_gate, b_branch_gate, w_out, norm_ffn,
         w_router_group, b_router_group, w_router_expert, b_router_expert, w_exp_gate, w_exp_up, w_exp_down,
         norm_final))
    laid = {
        **layout(x, norm_mix, w_in, w_branch_gate, b_branch_gate),
        "band": band_b(rel_bias), "mask": band_a(), "sinks": attn_sinks.reshape(HEADS),
        "w_mix": mix_slabs(w_o_a, w_o_b, w_out), "norm_ffn": norm_ffn.reshape(D),
        **router_layout(w_router_group, b_router_group, w_router_expert, b_router_expert),
        "w_exp_gate": w_exp_gate[0], "w_exp_up": w_exp_up[0], "w_exp_down": w_exp_down[0],
        "norm_final": norm_final,
    }
    nc = _bacc.Bacc("TRN2", target_bir_lowering=False, num_devices=1)
    arrays = {f"in_{name}_dram": np.ascontiguousarray(a) for name, a in laid.items()}
    args = {name: nc.dram_tensor(f"in_{name}_dram", a.shape, F32, kind="ExternalInput").ap()
            for name, a in laid.items()}
    out = nc.dram_tensor("out_0_dram", (SEQ, D), F32, kind="ExternalOutput").ap()
    encoder_block(nc, out=out, **args)
    r = _run(nc, [arrays], core_ids=[0])
    return r.results[0]["out_0_dram"].reshape(x.shape)
```
